# Optimizing a Trainium2 kernel written in Bass

```python
import math
import jax, jax.numpy as jnp
from jax import lax
import numpy as np

D_MODEL = 1024
BATCH = 1
SEQ = 256
DEPTH = 1
DEC_BATCH = 8
DEC_SEQ = 8
PAST_LEN = 2048
PAGE_SIZE = 128

RET_HEADS = 4
RET_DK = 128
RET_DV = 256
RET_QK = RET_HEADS * RET_DK
RET_V = RET_HEADS * RET_DV
ROPE_BASE = 10000.0
SSM_INNER = 2 * D_MODEL
SSM_HEADDIM = 64
SSM_HEADS = SSM_INNER // SSM_HEADDIM
SSM_GROUPS = 4
SSM_DSTATE = 128
CONV_WIDTH = 4
CONV_DIM = SSM_INNER + 2 * SSM_GROUPS * SSM_DSTATE
DT_MIN = 0.001
DT_MAX = 0.1
CHUNK = 128
N_EXPERTS = 32
TOP_K = 4
D_FF = D_MODEL
SWIGLU_LIMIT = 7.0
SWIGLU_ALPHA = 1.702
MOE_BLOCK = 128
EPS = 1e-6
IN_PROJ_DIM = 2 * RET_QK + 2 * RET_V + SSM_INNER + CONV_DIM + SSM_HEADS + 2 * D_MODEL

kernel_name = 'retnet_mamba2_gptoss_hybrid_step'

def rmsnorm(x, w):
    xf = x.astype(jnp.float32)
    y = xf * lax.rsqrt(jnp.mean(xf * xf, axis=-1, keepdims=True) + EPS)
    return (y * w.astype(jnp.float32)).astype(x.dtype)

def in_proj_splits():
    sizes = [RET_QK, RET_QK, RET_V, RET_V, SSM_INNER, CONV_DIM, SSM_HEADS, D_MODEL, D_MODEL]
    return [int(i) for i in np.cumsum(sizes)[:-1]]

def rotary(t, pos):
    half = RET_DK // 2
    inv_freq = 1.0 / (ROPE_BASE ** jnp.linspace(0.0, 1.0, half, dtype=jnp.float32))
    ang = pos.astype(jnp.float32)[:, None] * inv_freq[None, :]
    cos = jnp.cos(ang)[None, :, None, :]
    sin = jnp.sin(ang)[None, :, None, :]
    t1, t2 = t[..., :half], t[..., half:]
    return jnp.concatenate([t1 * cos - t2 * sin, t1 * sin + t2 * cos], axis=-1)

def retention_log_decay():
    return jnp.log(1.0 - 2.0 ** (-5.0 - jnp.arange(RET_HEADS, dtype=jnp.float32)))

def retention_chunked(q, k, v, s0):
    bsz, L = q.shape[:2]
    c = math.gcd(L, CHUNK)
    n = L // c
    lg = retention_log_decay()
    idx = jnp.arange(c, dtype=jnp.float32)
    diff = idx[:, None] - idx[None, :]
    decay_mask = jnp.where(diff >= 0, jnp.exp(lg[:, None, None] * jnp.maximum(diff, 0.0)), 0.0)
    q_decay = jnp.exp(lg[None, :] * (idx[:, None] + 1.0))[None, :, :, None]
    k_decay = jnp.exp(lg[None, :] * (c - 1.0 - idx[:, None]))[None, :, :, None]
    chunk_decay = jnp.exp(lg * c)[None, :, None, None]

    def to_chunks(t):
        return t.reshape(bsz, n, c, *t.shape[2:]).swapaxes(0, 1)

    def step(s, inp):
        qc, kc, vc = inp
        scores = jnp.einsum('bihd,bjhd->bhij', qc, kc) * decay_mask[None]
        o = jnp.einsum('bhij,bjhv->bihv', scores, vc)
        o = o + jnp.einsum('bihd,bhdv->bihv', qc * q_decay, s)
        s = s * chunk_decay + jnp.einsum('bjhd,bjhv->bhdv', kc * k_decay, vc)
        return s, o

    s, o = lax.scan(step, s0, (to_chunks(q), to_chunks(k), to_chunks(v)))
    return o.swapaxes(0, 1).reshape(bsz, L, RET_HEADS, RET_DV), s

def causal_conv(xbc, buf, w, b):
    L = xbc.shape[1]
    full = jnp.concatenate([buf, xbc], axis=1)
    out = b
    for i in range(CONV_WIDTH):
        out = out + full[:, i:i + L] * w[i]
    return jax.nn.silu(out), full[:, full.shape[1] - (CONV_WIDTH - 1):]

def ssd_chunked(xs, dt, bm, cm, a, h0):
    bsz, L = xs.shape[:2]
    c = math.gcd(L, CHUNK)
    n = L // c
    hpg = SSM_HEADS // SSM_GROUPS
    xg = xs.reshape(bsz, L, SSM_GROUPS, hpg, SSM_HEADDIM)
    dtg = dt.reshape(bsz, L, SSM_GROUPS, hpg)
    ag = a.reshape(SSM_GROUPS, hpg)
    causal = jnp.tril(jnp.ones((c, c), dtype=bool))[None, :, :, None, None]

    def to_chunks(t):
        return t.reshape(bsz, n, c, *t.shape[2:]).swapaxes(0, 1)

    def step(h, inp):
        xc, dtc, bc, cc = inp
        cum = jnp.cumsum(dtc * ag, axis=1)
        seg = cum[:, :, None] - cum[:, None, :]
        decay = jnp.exp(jnp.where(causal, seg, -jnp.inf))
        cb = jnp.einsum('bign,bjgn->bijg', cc, bc)
        wts = cb[..., None] * decay * dtc[:, None]
        y = jnp.einsum('bijgh,bjghp->bighp', wts, xc)
        y = y + jnp.einsum('bign,bghpn->bighp', cc, h) * jnp.exp(cum)[..., None]
        to_end = jnp.exp(cum[:, -1:] - cum) * dtc
        h = h * jnp.exp(cum[:, -1])[..., None, None] + jnp.einsum('bjgn,bjgh,bjghp->bghpn', bc, to_end, xc)
        return h, y

    hg0 = h0.reshape(bsz, SSM_GROUPS, hpg, SSM_HEADDIM, SSM_DSTATE)
    h, y = lax.scan(step, hg0, (to_chunks(xg), to_chunks(dtg), to_chunks(bm), to_chunks(cm)))
    y = y.swapaxes(0, 1).reshape(bsz, L, SSM_HEADS, SSM_HEADDIM)
    return y, h.reshape(bsz, SSM_HEADS, SSM_HEADDIM, SSM_DSTATE)

def mixer_block(x, pos, s_ret, s_ssm, s_conv, norm_mix, w_in, ret_norm, w_out_ret, conv_w, conv_b,
                dt_bias, a_log, d_skip, ssm_norm, w_out_ssm, w_out):
    f32 = jnp.float32
    bsz, L, _ = x.shape
    h = rmsnorm(x, norm_mix)
    proj = h @ w_in
    q, k, v, g_ret, z, xbc, dt_raw, g_a, g_b = jnp.split(proj, in_proj_splits(), axis=-1)
    q = rotary(q.astype(f32).reshape(bsz, L, RET_HEADS, RET_DK), pos)
    k = rotary(k.astype(f32).reshape(bsz, L, RET_HEADS, RET_DK), pos) * (RET_DK ** -0.5)
    v = v.astype(f32).reshape(bsz, L, RET_HEADS, RET_DV)
    o_ret, s_ret_new = retention_chunked(q, k, v, s_ret.astype(f32))
    o_ret = rmsnorm(o_ret, ret_norm).reshape(bsz, L, RET_V).astype(x.dtype)
    branch_a = (jax.nn.silu(g_ret) * o_ret) @ w_out_ret
    xbc_act, s_conv_new = causal_conv(xbc, s_conv.astype(x.dtype), conv_w, conv_b)
    xs, b_ssm, c_ssm = jnp.split(xbc_act.astype(f32), [SSM_INNER, SSM_INNER + SSM_GROUPS * SSM_DSTATE], axis=-1)
    dt = jax.nn.softplus(dt_raw.astype(f32) + dt_bias.astype(f32))
    a = -jnp.exp(a_log.astype(f32))
    xs_h = xs.reshape(bsz, L, SSM_HEADS, SSM_HEADDIM)
    y, s_ssm_new = ssd_chunked(xs_h, dt, b_ssm.reshape(bsz, L, SSM_GROUPS, SSM_DSTATE),
                               c_ssm.reshape(bsz, L, SSM_GROUPS, SSM_DSTATE), a, s_ssm.astype(f32))
    y = y + xs_h * d_skip.astype(f32)[:, None]
    y = y.reshape(bsz, L, SSM_INNER) * jax.nn.silu(z.astype(f32))
    y = rmsnorm(y.reshape(bsz, L, SSM_GROUPS, SSM_INNER // SSM_GROUPS),
                ssm_norm.reshape(SSM_GROUPS, SSM_INNER // SSM_GROUPS)).reshape(bsz, L, SSM_INNER).astype(x.dtype)
    branch_b = y @ w_out_ssm
    merged = jax.nn.sigmoid(g_a) * branch_a + jax.nn.sigmoid(g_b) * branch_b
    return merged @ w_out, s_ret_new, s_ssm_new, s_conv_new

def moe_ffn(h, w_router, b_router, w_gate_up, b_gate_up, w_down, b_down):
    bsz, L, d = h.shape
    x = h.reshape(-1, d)
    t = x.shape[0]
    logits = (x @ w_router + b_router).astype(jnp.float32)
    top_val, top_idx = lax.top_k(logits, TOP_K)
    gates = jax.nn.softmax(top_val, axis=-1).astype(x.dtype)
    n_assign = t * TOP_K
    e_flat = top_idx.reshape(-1).astype(jnp.int32)
    order = jnp.argsort(e_flat)
    e_sorted = e_flat[order]
    counts = jnp.bincount(e_flat, length=N_EXPERTS).astype(jnp.int32)
    starts = jnp.cumsum(counts) - counts
    padded = (counts + MOE_BLOCK - 1) // MOE_BLOCK * MOE_BLOCK
    pends = jnp.cumsum(padded)
    pstarts = pends - padded
    dest = pstarts[e_sorted] + jnp.arange(n_assign, dtype=jnp.int32) - starts[e_sorted]
    n_blocks = -(-(n_assign + N_EXPERTS * (MOE_BLOCK - 1)) // MOE_BLOCK)
    p = n_blocks * MOE_BLOCK
    tok_buf = jnp.full((p,), t, dtype=jnp.int32).at[dest].set((order // TOP_K).astype(jnp.int32))
    gate_buf = jnp.zeros((p,), x.dtype).at[dest].set(gates.reshape(-1)[order])
    block_start = jnp.arange(n_blocks, dtype=jnp.int32) * MOE_BLOCK
    block_expert = jnp.minimum(jnp.searchsorted(pends, block_start, side='right'), N_EXPERTS - 1)
    x_pad = jnp.concatenate([x, jnp.zeros((1, d), x.dtype)], axis=0)
    xb = x_pad[tok_buf].reshape(n_blocks, MOE_BLOCK, d)

    def expert_block(args):
        xblk, e = args
        gu = xblk @ w_gate_up[e] + b_gate_up[e]
        glu, lin = gu[:, :D_FF], gu[:, D_FF:]
        glu = jnp.minimum(glu, SWIGLU_LIMIT)
        lin = jnp.clip(lin, -SWIGLU_LIMIT, SWIGLU_LIMIT)
        act = glu * jax.nn.sigmoid(SWIGLU_ALPHA * glu) * (lin + 1.0)
        return act @ w_down[e] + b_down[e]

    yb = lax.map(expert_block, (xb, block_expert)).reshape(p, d)
    y = jnp.zeros((t + 1, d), x.dtype).at[tok_buf].add(yb * gate_buf[:, None])[:t]
    return y.reshape(bsz, L, d)

def setup_inputs(seed: int = 0) -> dict:
    key = jax.random.key(seed)
    ks = jax.random.split(key, 26)
    f32 = jnp.float32

    def nrm(k, shape, scale):
        return jax.random.normal(k, shape, f32) * scale

    x_prompt = nrm(ks[0], (BATCH, SEQ, D_MODEL), 1.0)
    x_sample = nrm(ks[1], (DEC_BATCH, DEC_SEQ, D_MODEL), 1.0)
    state_ret = nrm(ks[2], (DEPTH, DEC_BATCH, RET_HEADS, RET_DK, RET_DV), 0.5)
    state_ssm = nrm(ks[3], (DEPTH, DEC_BATCH, SSM_HEADS, SSM_HEADDIM, SSM_DSTATE), 0.1)
    state_conv = nrm(ks[4], (DEPTH, DEC_BATCH, CONV_WIDTH - 1, CONV_DIM), 1.0)
    norm_mix = 1.0 + nrm(ks[5], (DEPTH, D_MODEL), 0.02)
    w_in = nrm(ks[6], (DEPTH, D_MODEL, IN_PROJ_DIM), D_MODEL ** -0.5)
    ret_norm = 1.0 + nrm(ks[7], (DEPTH, RET_HEADS, RET_DV), 0.02)
    w_out_ret = nrm(ks[8], (DEPTH, RET_V, D_MODEL), RET_V ** -0.5)
    conv_w = nrm(ks[9], (DEPTH, CONV_WIDTH, CONV_DIM), CONV_WIDTH ** -0.5)
    conv_b = nrm(ks[10], (DEPTH, CONV_DIM), 0.02)
    dt0 = jnp.exp(jax.random.uniform(ks[11], (DEPTH, SSM_HEADS), f32, math.log(DT_MIN), math.log(DT_MAX)))
    dt_bias = dt0 + jnp.log(-jnp.expm1(-dt0))
    a_log = jnp.log(jax.random.uniform(ks[12], (DEPTH, SSM_HEADS), f32, 1.0, 16.0))
    d_skip = 1.0 + nrm(ks[13], (DEPTH, SSM_HEADS), 0.02)
    ssm_norm = 1.0 + nrm(ks[14], (DEPTH, SSM_INNER), 0.02)
    w_out_ssm = nrm(ks[15], (DEPTH, SSM_INNER, D_MODEL), SSM_INNER ** -0.5)
    w_out = nrm(ks[16], (DEPTH, D_MODEL, D_MODEL), D_MODEL ** -0.5)
    norm_ffn = 1.0 + nrm(ks[17], (DEPTH, D_MODEL), 0.02)
    w_router = nrm(ks[18], (DEPTH, D_MODEL, N_EXPERTS), D_MODEL ** -0.5)
    b_router = nrm(ks[19], (DEPTH, N_EXPERTS), 0.01)
    w_gate_up = nrm(ks[20], (DEPTH, N_EXPERTS, D_MODEL, 2 * D_FF), D_MODEL ** -0.5)
    b_gate_up = nrm(ks[21], (DEPTH, N_EXPERTS, 2 * D_FF), 0.01)
    w_down = nrm(ks[22], (DEPTH, N_EXPERTS, D_FF, D_MODEL), D_FF ** -0.5)
    b_down = nrm(ks[23], (DEPTH, N_EXPERTS, D_MODEL), 0.01)
    norm_final = 1.0 + nrm(ks[24], (D_MODEL,), 0.02)
    return {'x_prompt': x_prompt, 'x_sample': x_sample,
            'state_ret': state_ret, 'state_ssm': state_ssm, 'state_conv': state_conv,
            'norm_mix': norm_mix, 'w_in': w_in, 'ret_norm': ret_norm, 'w_out_ret': w_out_ret,
            'conv_w': conv_w, 'conv_b': conv_b, 'dt_bias': dt_bias, 'a_log': a_log, 'd_skip': d_skip,
            'ssm_norm': ssm_norm, 'w_out_ssm': w_out_ssm, 'w_out': w_out, 'norm_ffn': norm_ffn,
            'w_router': w_router, 'b_router': b_router, 'w_gate_up': w_gate_up, 'b_gate_up': b_gate_up,
            'w_down': w_down, 'b_down': b_down, 'norm_final': norm_final}

def reference(x_prompt, x_sample, state_ret, state_ssm, state_conv, norm_mix, w_in, ret_norm, w_out_ret,
              conv_w, conv_b, dt_bias, a_log, d_skip, ssm_norm, w_out_ssm, w_out, norm_ffn,
              w_router, b_router, w_gate_up, b_gate_up, w_down, b_down, norm_final):
    def trunk(x, pos, ret_states, ssm_states, conv_states):
        new_ret, new_ssm, new_conv = [], [], []
        for l in range(DEPTH):
            mix, sr, ss, sc = mixer_block(x, pos, ret_states[l], ssm_states[l], conv_states[l],
                                          norm_mix[l], w_in[l], ret_norm[l], w_out_ret[l], conv_w[l], conv_b[l],
                                          dt_bias[l], a_log[l], d_skip[l], ssm_norm[l], w_out_ssm[l], w_out[l])
            x = x + mix
            x = x + moe_ffn(rmsnorm(x, norm_ffn[l]), w_router[l], b_router[l], w_gate_up[l], b_gate_up[l],
                            w_down[l], b_down[l])
            new_ret.append(sr)
            new_ssm.append(ss)
            new_conv.append(sc)
        return rmsnorm(x, norm_final), jnp.stack(new_ret), jnp.stack(new_ssm), jnp.stack(new_conv)

    bp = x_prompt.shape[0]
    zeros_ret = jnp.zeros((DEPTH, bp, RET_HEADS, RET_DK, RET_DV), jnp.float32)
    zeros_ssm = jnp.zeros((DEPTH, bp, SSM_HEADS, SSM_HEADDIM, SSM_DSTATE), jnp.float32)
    zeros_conv = jnp.zeros((DEPTH, bp, CONV_WIDTH - 1, CONV_DIM), x_prompt.dtype)
    pos_prompt = jnp.arange(x_prompt.shape[1], dtype=jnp.int32)
    pos_sample = PAST_LEN + jnp.arange(x_sample.shape[1], dtype=jnp.int32)
    y_prompt, ret_p, ssm_p, conv_p = trunk(x_prompt, pos_prompt, zeros_ret, zeros_ssm, zeros_conv)
    y_sample, ret_s, ssm_s, conv_s = trunk(x_sample, pos_sample, state_ret, state_ssm, state_conv)
    return (y_prompt, y_sample, ret_p, ret_s, ssm_p, ssm_s, conv_p, conv_s)


_drawn_inputs = setup_inputs


def setup_inputs(seed=0):
    import zlib

    import numpy as np

    out = dict(_drawn_inputs(seed))
    spreads = {}
    factors = {'ret_norm': 3.074, 'b_gate_up': 8.0, 'b_down': 8.0, 'norm_final': 2.848}
    for name, (base, spread) in spreads.items():
        noise = np.random.default_rng([zlib.crc32(name.encode()), seed]).standard_normal(out[name].shape)
        drawn = base * np.exp(spread * noise) if base else spread * noise
        out[name] = __import__('jax').numpy.asarray(drawn.astype(out[name].dtype))
    for name, factor in factors.items():
        out[name] = (out[name] * factor).astype(out[name].dtype)
    return out
```

```python
from contextlib import ExitStack, contextmanager
import math

import numpy as np

import concourse.bass as bass
from concourse import mybir

F32 = mybir.dt.float32
BF16 = mybir.dt.bfloat16
I32 = mybir.dt.int32
U32 = mybir.dt.uint32
ALU = mybir.AluOpType
ACT = mybir.ActivationFunctionType
AX = mybir.AxisListType

P = 128
D_MODEL = 1024
SEQ, DEC_BATCH, DEC_SEQ, PAST_LEN = 256, 8, 8, 2048
TOKENS = SEQ + DEC_BATCH * DEC_SEQ
TILES = 3
ROWS = (128, 128, 64)
TOK0 = (0, 128, 256)
SAMPLE = slice(SEQ, TOKENS)
NS = DEC_BATCH * DEC_SEQ
RET_HEADS, RET_DK, RET_DV = 4, 128, 256
SSM_HEADS, HEADDIM, GROUPS, DSTATE = 32, 64, 4, 128
HPG = SSM_HEADS // GROUPS
GW = HPG * HEADDIM
INNER = SSM_HEADS * HEADDIM
CONV_DIM = INNER + 2 * GROUPS * DSTATE
TAPS = 4
N_EXPERTS, TOP_K, D_FF = 32, 4, 1024
LIMIT, ALPHA = 7.0, 1.702
EPS = 1e-6
KT = D_MODEL // P
CH = 512
COL_Q, COL_V, COL_G, COL_Z = 0, 1024, 2048, 3072
COL_XBC = COL_Z + INNER
COL_DT = COL_XBC + CONV_DIM
COL_GATES = COL_DT + SSM_HEADS
MAX_BLOCKS = (TOKENS * TOP_K - N_EXPERTS) // P + N_EXPERTS
BLOCK_COLS = MAX_BLOCKS + 2
NOWHERE = float(1 << 20)
NEG = -1.0e30
PROMPT_RAW = TAPS - 1 + SEQ
SAMPLE_RAW = DEC_BATCH * (TAPS - 1 + DEC_SEQ)
RAW = PROMPT_RAW + 1 + SAMPLE_RAW


def constants():
    f = np.float32
    i, j = np.meshgrid(np.arange(P), np.arange(P))
    js, is_ = j[:NS, :NS], i[:NS, :NS]
    same = js // DEC_SEQ == is_ // DEC_SEQ
    gamma = 1.0 - 2.0 ** (-5.0 - np.arange(RET_HEADS))
    lg = np.log(gamma)
    scale = RET_DK ** -0.5

    def rows(a):
        out = np.zeros((P, a.shape[1]), f)
        out[:a.shape[0]] = a
        return out

    inv = 1.0 / (10000.0 ** np.linspace(0.0, 1.0, RET_DK // 2, dtype=f))
    pos = np.zeros((TILES, P))
    pos[0], pos[1] = np.arange(P), np.arange(P) + P
    pos[2, :NS] = PAST_LEN + np.arange(NS) % DEC_SEQ
    ang = (pos.astype(f)[:, :, None] * inv.astype(f)[None, None, :]).astype(f).astype(np.float64)
    loc = np.arange(NS) % DEC_SEQ
    parts = {
        "ident": np.eye(P),
        "upto": (j <= i),
        "before": (j < i),
        "ones": np.ones((P, P)),
        "upto_s": rows((js <= is_) & same),
        "ones_s": rows(same),
        "mask": np.where(i >= j, 0.0, NEG),
        "mask_s": rows(np.where((is_ >= js) & same, 0.0, NEG)),
        "decay": np.concatenate([np.where(i >= j, np.exp(lg[h] * np.maximum(i - j, 0)), 0.0) * scale
                                 for h in range(RET_HEADS)], 1),
        "decay_s": rows(np.concatenate([np.where((is_ >= js) & same, np.exp(lg[h] * np.maximum(is_ - js, 0)), 0.0)
                                        * scale for h in range(RET_HEADS)], 1)),
        "q_decay": np.tile(np.concatenate([np.exp(lg[h] * (np.concatenate([np.arange(P), loc]) + 1.0))
                                           for h in range(RET_HEADS)])[None], (P, 1)),
        "seq_cols": np.tile((np.arange(DEC_BATCH)[:, None] == np.arange(NS)[None] // DEC_SEQ).reshape(1, -1), (P, 1)),
        "cos": np.concatenate(list(np.cos(ang)), 1),
        "sin": np.concatenate(list(np.sin(ang)), 1),
        "k_decay": np.exp(lg[None] * (P - 1.0 - np.arange(P)[:, None])) * scale,
        "k_decay_s": rows(np.exp(lg[None] * (DEC_SEQ - 1.0 - loc[:, None])) * scale),
        "seq_rows": rows(np.arange(NS)[:, None] // DEC_SEQ == np.arange(DEC_BATCH)[None]),
        "experts": np.tile(np.arange(N_EXPERTS)[None], (P, 1)),
        "blocks": np.tile(np.arange(BLOCK_COLS)[None], (P, 1)),
        "assign": np.concatenate([(TOK0[t] + np.arange(P))[:, None] * TOP_K + np.arange(TOP_K)[None] + 1
                                  for t in range(TILES)], 1),
        "lanes": np.tile(np.arange(P)[None], (P, 1)),
        "mod32": (np.arange(P) % N_EXPERTS)[:, None],
    }
    at, n = {}, 0
    for name, a in parts.items():
        at[name] = n
        n += a.shape[1]
    return np.ascontiguousarray(np.concatenate([np.asarray(a, f) for a in parts.values()], 1)), at, n


RET_GAMMA = [1.0 - 2.0 ** (-5.0 - h) for h in range(RET_HEADS)]


class Chain:

    def __init__(self, eng, sem):
        self.eng, self.sem, self.n, self.at = eng, sem, 0, 0

    def link(self, ins):
        ins.then_inc(self.sem, 1)
        self.n += 1
        self.eng.wait_ge(self.sem, self.at + self.n)

    @contextmanager
    def fori(self, count, links):
        with self.eng.Fori(0, count) as i:
            first = self.n
            self.at = i * links
            yield i
            assert self.n - first == links, (self.n - first, links)
        if isinstance(count, int):
            self.at = 0
            self.n += links * (count - 1)
        else:
            self.at = (count - 1) * links


def program(nc, x_all, cst, parc, rowp, norm_final, w_in, w_out_ret, w_out_ssm, w_out, w_router,
            ret_in, ssm_in, w_gate_up, b_gate_up, w_down, b_down,
            y_out, ret_p, ret_s, ssm_p, ssm_s, conv_p, conv_s):
    _, C, CW = constants()
    with ExitStack() as ctx:
        def sb(name, shape, dt=F32):
            return ctx.enter_context(nc.sbuf_tensor(name, shape, dt))

        def sem(name):
            return ctx.enter_context(nc.semaphore(name))

        CST = sb("CST", [P, CW])
        X = sb("X", [P, TILES, D_MODEL])
        PARC = sb("PARC", [P, 24 * TAPS + 24 + 16 + 8 + 8 + 8 + 24 * 24])
        ROWP = sb("ROWP", [P, 4, 32])
        WDT = sb("WDT", [P, KT, SSM_HEADS])
        WR = sb("WR", [P, KT, N_EXPERTS])
        ARENA = sb("ARENA", [P, 38656])
        TEMPS = sb("TEMPS", [P, 4608])
        SMALL = sb("SMALL", [P, 1472])

        def const(name, width, r=P, start=0):
            return CST[0:r, C[name] + start:C[name] + start + width]

        o = 0
        conv_w = PARC[:, o:o + 96].rearrange("p (m i) -> p m i", i=TAPS)
        o += 96
        conv_b = PARC[:, o:o + 24]
        o += 24
        ssm_norm = PARC[:, o:o + 16]
        o += 16
        ret_norm = PARC[:, o:o + 8]
        o += 8
        norm_mix = PARC[:, o:o + 8]
        o += 8
        norm_ffn = PARC[:, o:o + 8]
        o += 8
        conv_state = PARC[:, o:o + 576].rearrange("p (m b i) -> p m b i", b=DEC_BATCH, i=TAPS - 1)
        dt_bias, a_log, d_skip, b_router = (ROWP[:, n, :] for n in range(4))

        def region(a, n):
            return ARENA[:, a:a + n]

        W = [region(4096 * s, 4096).rearrange("p (k n) -> p k n", k=KT) for s in range(2)]
        W16 = [region(4096 * s, 4096).rearrange("p (k n) -> p k n", k=2 * KT) for s in range(2)]
        HT = region(8192, 2560).rearrange("p (k n) -> p k n", k=KT)
        XBC = region(10752, 24 * TOKENS).rearrange("p (m n) -> p m n", m=24)
        QKV = region(18432, 6144).rearrange("p (t n) -> p t n", t=TILES)
        XS = region(24576, 6144).rearrange("p (t n) -> p t n", t=TILES)
        BTOK = region(30720, 1536).rearrange("p (t n) -> p t n", t=TILES)
        QKT = region(32256, 2560).rearrange("p (h n) -> p h n", h=2 * RET_HEADS)
        QTD = region(34816, 768).rearrange("p (h n) -> p h n", h=RET_HEADS)
        O = region(35584, 3072).rearrange("p (t n) -> p t n", t=TILES)
        H = region(24576, 3072).rearrange("p (t n) -> p t n", t=TILES)
        RAWB = region(35584, 2 * 4 * RAW).rearrange("p (s m n) -> p s m n", s=2, m=4)
        SSM_IN = [region(3072 * s, 2048) for s in range(2)]
        RET_IN = [region(3072 * s + 2048, 1024) for s in range(2)]
        SSM_PR = region(6144, 2048)
        XDT = region(10752, 2048)
        XEND = region(12800, 2048)
        RET_PR = region(14848, 1024)
        YT = region(10752, 5120).rearrange("p (k n) -> p k n", k=16)
        OT = region(15872, 2560).rearrange("p (k n) -> p k n", k=8)
        SG = region(18432, 5120).rearrange("p (m n) -> p m n", m=16)
        MERGED = region(32256, 2560).rearrange("p (k n) -> p k n", k=KT)

        ROT = TEMPS[:, 0:2048].rearrange("p (a n) -> p a n", a=4)
        SEG = TEMPS[:, 0:2048].rearrange("p (s h n) -> p s h n", s=2, h=HPG)
        CTM = [TEMPS[:, 1536 * s:1536 * s + 256].rearrange("p (g n) -> p g n", g=4) for s in range(2)]
        QTM = [TEMPS[:, 1536 * s + 256:1536 * s + 512].rearrange("p (g n) -> p g n", g=4) for s in range(2)]
        BM = [TEMPS[0:NS, 1536 * s + 512:1536 * s + 1024] for s in range(2)]
        KM = [TEMPS[0:NS, 1536 * s + 1024:1536 * s + 1536] for s in range(2)]
        TMP = TEMPS[:, 3072:3584]
        KDEC = TEMPS[:, 3584:4096]
        SM = TEMPS[:, 4096:4608].rearrange("p (h n) -> p h n", h=RET_HEADS)
        SIL = [TEMPS[:, 3584 + 512 * s:4096 + 512 * s] for s in range(2)]
        SQ = TEMPS[:, 0:1024]

        o = 0

        def small(n):
            nonlocal o
            o += n
            assert o <= 1472
            return SMALL[:, o - n:o]

        RMS = small(32)
        DTW = small(96 * 6).rearrange("p (a n) -> p a n", a=6)
        DT, DTA, CUM, ECUM, TOEND, LNW = (DTW[:, n, :].rearrange("p (t h) -> p t h", t=TILES) for n in range(6))
        NA = small(32)
        DEC_P = small(32)
        DEC_S = small(256).rearrange("p (b h) -> p b h", b=DEC_BATCH)
        CONV_TAIL = small(24 * 3).rearrange("p (m i) -> p m i", i=3)
        CONV_TAIL_S = PARC[:, 160:160 + 576].rearrange("p (m b i) -> p m b i", b=DEC_BATCH, i=TAPS - 1)

        PS = [ctx.enter_context(nc.psum_tensor(f"PS{n}", [P, 512], F32)) for n in range(8)]
        s_x, s_cst, s_par, s_wdt = sem("x_in"), sem("constants_in"), sem("parameters_in"), sem("w_dt_in")
        s_w = [sem(f"weights_in_{s}") for s in range(2)]
        s_st_in = [sem(f"states_in_{s}") for s in range(2)]
        s_st_out = [sem(f"states_out_{s}") for s in range(2)]
        s_small_out = sem("small_out")
        dve_order, act_order, pool_order = sem("dve_order"), sem("act_order"), sem("pool_order")
        rms_init = sem("rms_init")
        squares, variance, deviation = sem("squares"), sem("variance"), sem("deviation")
        h_ready, h_turned, ht_ready = sem("h_ready"), sem("h_turned"), sem("ht_ready")
        xbc_mm, raw_ready, pads_ready, tails_done, conv_done = (
            sem("xbc_mm"), sem("raw_ready"), sem("pads_ready"), sem("tails_done"), sem("conv_done"))
        silu_xbc = sem("silu_xbc")
        dt_mm, dt_arg, dt_exp, dt_w, dt_ln, na_ready, dta_ready = (
            sem("dt_mm"), sem("dt_arg"), sem("dt_exp"), sem("dt_w"), sem("dt_ln"), sem("na_ready"), sem("dta_ready"))
        qkv_mm, qkv_evac, rotated = sem("qkv_mm"), sem("qkv_evac"), sem("rotated")
        turn_mm, turn_evac = sem("turn_mm"), sem("turn_evac")
        cum_mm, cum_read, cum_exp, toend_ready = sem("cum_mm"), sem("cum_read"), sem("cum_exp"), sem("toend_ready")
        seg_mm, seg_sub, seg_exp, wts_ready = sem("seg_mm"), sem("seg_sub"), sem("seg_exp"), sem("wts_ready")
        xdt_ready, back_mm, y_evac = sem("xdt_ready"), sem("back_mm"), sem("y_evac")
        qtd_ready, kdec_ready = sem("qtd_ready"), sem("kdec_ready")
        score_mm, score_ready, ret_mm, ret_evac = sem("score_mm"), sem("score_ready"), sem("ret_mm"), sem("ret_evac")
        zero_ready = sem("zero_ready")
        masks_ready, cross_mm, upd_mm, upd_evac, closed = (
            sem("masks_ready"), sem("cross_mm"), sem("upd_mm"), sem("upd_evac"), sem("closed"))
        sample_y = sem("sample_y")
        g_mm, z_mm, sil_ready, sil_used = sem("g_mm"), sem("z_mm"), sem("sil_ready"), sem("sil_used")
        gate_mm, gate_evac = sem("gate_mm"), sem("gate_evac")
        y_scaled, turn2_mm, turn2_evac = sem("y_scaled"), sem("turn2_mm"), sem("turn2_evac")
        oa_mm, oa_evac, ob_mm, ob_evac, out_mm, x1_ready = (
            sem("oa_mm"), sem("oa_evac"), sem("ob_mm"), sem("ob_evac"), sem("out_mm"), sem("x1_ready"))

        ZERO = small(256)[0:1, :].bitcast(BF16)
        UNITS = [(t, g) for t in range(TILES) for g in range(GROUPS)]

        def heads(ap, n, width):
            return ap.unsqueeze(2).to_broadcast([ap.shape[0], n, width])

        def seg_bank(u, half):
            return PS[2 * (u % 2) + half]

        def quads(bank):
            return bank[:, :].rearrange("p (q n) -> p q n", q=4)

        def w_cols(w, start, width=CH):
            return w[:, start:start + width].rearrange("(k p) n -> p k n", p=P)

        def w_ds(w, at, width=CH):
            return w[:, bass.ds(at, width)].rearrange("(k p) n -> p k n", p=P)

        def sync_mixer(sp):
            sp.dma_start(X[:, 0:2, :], x_all[0:SEQ, :].rearrange("(t p) d -> p t d", p=P)).then_inc(s_x, 16)
            sp.dma_start(X[0:NS, 2, :], x_all[SAMPLE, :]).then_inc(s_x, 16)
            sp.dma_start(CST[:, :], cst).then_inc(s_cst, 16)
            sp.dma_start(PARC[:, :], parc).then_inc(s_par, 16)
            sp.dma_start(ROWP[:, :, :].rearrange("p a b -> p (a b)"), rowp.to_broadcast([P, 128])).then_inc(s_par, 16)
            sp.dma_start(WDT[:, :, :], w_cols(w_in, COL_DT, SSM_HEADS)).then_inc(s_wdt, 16)
            sp.dma_start(WR[:, :, :], w_cols(w_router, 0, N_EXPERTS)).then_inc(s_wdt, 16)

            def stream(col, rounds, used, per_chunk, before):
                for s in range(2):
                    if before is not None:
                        sp.wait_ge(*before[s])
                    sp.dma_start(W[s], w_cols(w_in, col + CH * s)).then_inc(s_w[s], 16)
                if rounds > 1:
                    with sp.Fori(0, rounds - 1) as j:
                        for s in range(2):
                            sp.wait_ge(used, j * (2 * per_chunk) + per_chunk * (s + 1))
                            sp.dma_start(W[s], w_ds(w_in, j * (2 * CH) + (col + CH * (s + 2)))).then_inc(s_w[s], 16)

            stream(COL_XBC, 3, xbc_mm, 4, None)
            stream(COL_Q, 2, qkv_mm, 3, [(xbc_mm, 20), (xbc_mm, 24)])
            sp.wait_ge(qkv_mm, 12)

            def state_in(p, ssm, ret):
                sp.dma_start(SSM_IN[p], ssm).then_inc(s_st_in[p], 16)
                sp.dma_start(RET_IN[p].rearrange("p (h n) -> p h n", h=RET_HEADS), ret).then_inc(s_st_in[p], 16)

            def state_out(p, ssm, ret):
                sp.dma_start(ssm, SSM_IN[p]).then_inc(s_st_out[p], 16)
                sp.dma_start(ret, RET_IN[p].rearrange("p (h n) -> p h n", h=RET_HEADS)).then_inc(s_st_out[p], 16)

            for p in range(2):
                state_in(p, ssm_in[p], ret_in[p].rearrange("h d v -> d h v"))
            sp.wait_ge(tails_done, 8 + 24)
            sp.dma_start(conv_p, CONV_TAIL).then_inc(s_small_out, 16)
            sp.dma_start(conv_s, CONV_TAIL_S).then_inc(s_small_out, 16)
            sp.wait_ge(y_evac, 8)
            sp.dma_start(ssm_p, SSM_PR).then_inc(s_small_out, 16)
            sp.wait_ge(ret_evac, 4)
            sp.dma_start(ret_p.rearrange("h d v -> d h v"),
                         RET_PR.rearrange("p (h n) -> p h n", h=RET_HEADS)).then_inc(s_small_out, 16)
            ssm_i = ssm_in.rearrange("b n q -> n b q")
            ret_i = ret_in.rearrange("b h d v -> d b h v")
            ssm_o = ssm_s.rearrange("b n q -> n b q")
            ret_o = ret_s.rearrange("b h d v -> d b h v")
            with sp.Fori(0, DEC_BATCH // 2 - 1) as j:
                for p in range(2):
                    sp.wait_ge(upd_evac, j * 12 + (6 * p + 8))
                    state_out(p, ssm_o[:, bass.ds(j * 2 + p, 1), :].squeeze(1),
                              ret_o[:, bass.ds(j * 2 + p, 1), :, :].squeeze(1))
                    sp.wait_ge(s_st_out[p], j * 32 + 32)
                    state_in(p, ssm_i[:, bass.ds(j * 2 + (p + 2), 1), :].squeeze(1),
                             ret_i[:, bass.ds(j * 2 + (p + 2), 1), :, :].squeeze(1))
            for p in range(2):
                b = DEC_BATCH - 2 + p
                sp.wait_ge(upd_evac, 6 * (b + 1) + 2)
                state_out(p, ssm_s[b], ret_s[b].rearrange("h d v -> d h v"))
            for p in range(2):
                sp.wait_ge(s_st_out[p], 32 * (DEC_BATCH // 2))
            sp.wait_ge(s_small_out, 64)
            stream(COL_G, 1, None, 3, None)
            stream(COL_Z, 2, z_mm, 3, [(g_mm, 3), (g_mm, 6)])
            stream(COL_GATES, 2, gate_mm, 4, [(z_mm, 9), (z_mm, 12)])
            for s in range(2):
                sp.wait_ge(gate_mm, 12 + 4 * s)
                sp.dma_start(W[s], w_cols(w_out_ret, CH * s)).then_inc(s_w[s], 16)
            for s in range(2):
                sp.wait_ge(oa_mm, 4 + 4 * s)
                sp.dma_start(W16[s], w_cols(w_out_ssm, 256 * s, 256)).then_inc(s_w[s], 16)
            for s in range(2):
                sp.wait_ge(ob_mm, 2 + 2 * s)
                sp.dma_start(W16[s], w_cols(w_out_ssm, 256 * (s + 2), 256)).then_inc(s_w[s], 16)
            for s in range(2):
                sp.wait_ge(ob_mm, 6 + 2 * s)
                sp.dma_start(W[s], w_cols(w_out, CH * s)).then_inc(s_w[s], 16)

        def tensor_mixer(pe):
            pe.wait_ge(s_cst, 16)
            ident = const("ident", P)
            for n in range(6):
                t, k0 = n // 2, 4 * (n % 2)
                r = ROWS[t]
                pe.wait_ge(h_ready, t + 1)
                for k in range(4):
                    mm = pe.transpose(quads(PS[n])[:, k, 0:r], H[0:r, t, P * (k0 + k):P * (k0 + k + 1)],
                                      const("ident", r, r))
                mm.then_inc(h_turned, 1)
            pe.wait_ge(ht_ready, 6)

            with pe.Fori(0, 3) as j:
                for s in range(2):
                    pe.wait_ge(s_w[s], j * 16 + 16)
                    for m in range(4):
                        pe.wait_ge(raw_ready, j * 8 + (4 * s + m + 1))
                        for k in range(KT):
                            mm = pe.matmul(PS[4 * s + m][:, 0:TOKENS], W[s][:, k, P * m:P * (m + 1)], HT[:, k, :],
                                           start=(k == 0), stop=(k == KT - 1))
                        mm.then_inc(xbc_mm, 1)

            def by_token(bank, s, t, width, w):
                r = ROWS[t]
                for k in range(KT):
                    mm = pe.matmul(bank[0:r, 0:width], HT[:, k, TOK0[t]:TOK0[t] + r], w[:, k, :],
                                   start=(k == 0), stop=(k == KT - 1))
                return mm

            pe.wait_ge(raw_ready, 8 + 24)
            pe.wait_ge(s_wdt, 32)
            for t in range(TILES):
                mm = by_token(PS[3][:, 32 * t:32 * t + 32], 0, t, 32, WDT)
            mm.then_inc(dt_mm, 1)
            with pe.Fori(0, 2) as j:
                for s in range(2):
                    pe.wait_ge(s_w[s], j * 16 + 64)
                    for t in range(TILES):
                        pe.wait_ge(qkv_evac, j * 6 + (3 * s + t + 1))
                        by_token(PS[4 * s + t], s, t, CH, W[s]).then_inc(qkv_mm, 1)

            def running_sums():
                pe.wait_ge(dta_ready, 1)
                bank = PS[3]
                for t in range(TILES):
                    r = ROWS[t]
                    upto, ones = (("upto", "ones"), ("upto_s", "ones_s"))[t == 2]
                    pe.matmul(bank[0:r, 32 * t:32 * t + 32], const(upto, r, r), DTA[0:r, t, :], start=True, stop=True)
                    pe.matmul(bank[0:r, 96 + 32 * t:128 + 32 * t], const(ones, r, r), DTA[0:r, t, :],
                              start=True, stop=True)
                for b in range(DEC_BATCH):
                    mm = pe.matmul(bank[:, 192 + 32 * b:224 + 32 * b],
                                   const("seq_rows", 1, NS, b).to_broadcast([NS, P]), DTA[0:NS, 2, :],
                                   start=True, stop=True)
                mm.then_inc(cum_mm, 1)

            pe.wait_ge(qkv_evac, 6 + 12)
            pe.wait_ge(silu_xbc, 2)
            for n in range(21):
                if n >= 4:
                    pe.wait_ge(turn_evac, n - 3)
                bank = PS[4 + n % 4]
                if n < 15:
                    t, m0 = (n // 4, 4 * (n % 4)) if n < 12 else (n - 12, 16)
                    r = ROWS[t]
                    for m in range(4):
                        mm = pe.transpose(bank[0:r, P * m:P * (m + 1)], XBC[:, m0 + m, TOK0[t]:TOK0[t] + r], ident)
                else:
                    if n == 15:
                        running_sums()
                    t, half = (n - 15) // 2, (n - 15) % 2
                    r = ROWS[t]
                    pe.wait_ge(rotated, t + 1)
                    for h in range(RET_HEADS):
                        mm = pe.transpose(quads(bank)[:, h, 0:r],
                                          QKV[0:r, t, 512 * half + P * h:512 * half + P * (h + 1)],
                                          const("ident", r, r))
                mm.then_inc(turn_mm, 1)

            def front(u):
                t, g = UNITS[u]
                r = ROWS[t]
                tok = slice(TOK0[t], TOK0[t] + r)
                upto = const("upto_s" if t == 2 else "upto", r, r)
                if u >= 2:
                    pe.wait_ge(wts_ready, u - 1)
                pe.matmul(PS[4][0:r, P * (u % 2):P * (u % 2) + r], XBC[:, 16 + g, tok], XBC[:, 20 + g, tok],
                          start=True, stop=True)
                for h in range(HPG):
                    mm = pe.matmul(quads(seg_bank(u, h // 4))[0:r, h % 4, 0:r],
                                   DTA[0:r, t, HPG * g + h:HPG * g + h + 1].to_broadcast([r, r]), upto,
                                   start=True, stop=True)
                    if h % 4 == 3:
                        mm.then_inc(seg_mm, 1)

            def back(u):
                t, g = UNITS[u]
                r = ROWS[t]
                cols = slice(GW * g, GW * (g + 1))
                pe.wait_ge(wts_ready, u + 1)
                pe.wait_ge(xdt_ready, u + 1)
                if u >= 1:
                    pe.wait_ge(y_evac, u)
                for h in range(HPG):
                    at = GW * g + HEADDIM * h
                    mm = pe.matmul(PS[5][0:r, HEADDIM * h:HEADDIM * (h + 1)], SEG[0:r, u % 2, h, 0:r],
                                   XDT[0:r, at:at + HEADDIM], start=True, stop=True)
                if t == 1:
                    pe.matmul(PS[6][0:r, :], XBC[:, 20 + g, P:2 * P], SSM_PR[:, cols], start=True, stop=True)
                if t < 2:
                    mm = pe.matmul(PS[7][:, :], BTOK[0:r, t, P * g:P * (g + 1)], XEND[0:r, cols],
                                   start=True, stop=True)
                mm.then_inc(back_mm, 1)

            pe.wait_ge(cum_read, 1)
            pe.wait_ge(turn_evac, 21)
            front(0)
            for u in range(len(UNITS)):
                if u + 1 < len(UNITS):
                    front(u + 1)
                back(u)

            def scores(t, bank):
                r = ROWS[t]
                tok = slice(TOK0[t], TOK0[t] + r)
                for h in range(RET_HEADS):
                    mm = pe.matmul(quads(bank)[0:r, h, 0:r], QKT[:, RET_HEADS + h, tok], QKT[:, h, tok],
                                   start=True, stop=True)
                mm.then_inc(score_mm, 1)

            def retain(t, banks, carried, open_end):
                r = ROWS[t]
                pe.wait_ge(score_ready, t + 1)
                for h in range(RET_HEADS):
                    out = banks[h // 2][0:r, RET_DV * (h % 2):RET_DV * (h % 2 + 1)]
                    v = QKV[0:r, t, 1024 + RET_DV * h:1024 + RET_DV * (h + 1)]
                    if open_end:
                        mm = pe.matmul(out, SM[0:r, h, 0:r], v, start=(h % 2 == 0), stop=False,
                                       skip_group_check=True)
                        continue
                    mm = pe.matmul(out, SM[0:r, h, 0:r], v, start=True, stop=not carried)
                    if carried:
                        mm = pe.matmul(out, QTD[:, h, 0:P], RET_PR[:, RET_DV * h:RET_DV * (h + 1)],
                                       start=False, stop=True)
                mm.then_inc(ret_mm, 1)

            def keep(t):
                pe.wait_ge(kdec_ready, t + 1)
                for h in range(RET_HEADS):
                    mm = pe.matmul(PS[3 + h // 2][:, RET_DV * (h % 2):RET_DV * (h % 2 + 1)],
                                   KDEC[:, P * h:P * (h + 1)],
                                   QKV[:, t, 1024 + RET_DV * h:1024 + RET_DV * (h + 1)], start=True, stop=True)
                mm.then_inc(ret_mm, 1)

            pe.wait_ge(y_evac, 12)
            pe.wait_ge(qtd_ready, 1)
            scores(0, PS[0])
            scores(1, PS[5])
            retain(0, (PS[1], PS[2]), False, False)
            keep(0)
            pe.wait_ge(ret_evac, 2)
            retain(1, (PS[6], PS[7]), True, False)
            keep(1)
            scores(2, PS[5])
            pe.wait_ge(ret_evac, 3)
            retain(2, (PS[0], PS[1]), False, True)

            pe.wait_ge(ret_evac, 4)
            pe.wait_ge(zero_ready, 1)
            for g in range(GROUPS):
                pe.matmul(PS[2 + g][0:NS, :], ZERO[:, 0:NS], ZERO[:, :], start=True, stop=False,
                          skip_group_check=True)
            with pe.Fori(0, DEC_BATCH // 2) as j:
                for p in range(2):
                    pe.wait_ge(masks_ready, j * 2 + (p + 1))
                    pe.wait_ge(s_st_in[p], j * 32 + 32)
                    for g in range(GROUPS):
                        pe.matmul(PS[2 + g][0:NS, :], CTM[p][:, g, :], SSM_IN[p][:, GW * g:GW * (g + 1)],
                                  start=False, stop=False, skip_group_check=True)
                    for h in range(RET_HEADS):
                        mm = pe.matmul(PS[h // 2][0:NS, RET_DV * (h % 2):RET_DV * (h % 2 + 1)], QTM[p][:, h, :],
                                       RET_IN[p][:, RET_DV * h:RET_DV * (h + 1)],
                                       start=False, stop=False, skip_group_check=True)
                    mm.then_inc(cross_mm, 1)
                    for u in range(6):
                        bank = PS[6 + u % 2]
                        pe.wait_ge(upd_evac, j * 12 + (6 * p + u + 1))
                        if u < 4:
                            mm = pe.matmul(bank[:, :], BM[p][:, P * u:P * (u + 1)],
                                           XEND[0:NS, GW * u:GW * (u + 1)], start=True, stop=True)
                        else:
                            for e in range(2):
                                h = 2 * (u - 4) + e
                                mm = pe.matmul(bank[:, RET_DV * e:RET_DV * (e + 1)], KM[p][:, P * h:P * (h + 1)],
                                               QKV[0:NS, 2, 1024 + RET_DV * h:1024 + RET_DV * (h + 1)],
                                               start=True, stop=True)
                        mm.then_inc(upd_mm, 1)
            for n in range(6):
                mm = pe.matmul(PS[n][0:NS, :], ZERO[:, 0:NS], ZERO[:, :], start=False, stop=True,
                               skip_group_check=True)
            mm.then_inc(closed, 1)

            pe.wait_ge(sample_y, 1)
            for s in range(2):
                pe.wait_ge(s_w[s], 16 * 6)
                for t in range(TILES):
                    by_token(PS[4 * s + t], s, t, CH, W[s]).then_inc(g_mm, 1)
            with pe.Fori(0, 2) as j:
                for s in range(2):
                    pe.wait_ge(s_w[s], j * 16 + 16 * 7)
                    for t in range(TILES):
                        pe.wait_ge(sil_ready, j * 6 + (3 * s + t + 1))
                        by_token(PS[4 * s + t], s, t, CH, W[s]).then_inc(z_mm, 1)
            pe.wait_ge(sil_ready, 18)
            with pe.Fori(0, 2) as j:
                for s in range(2):
                    pe.wait_ge(s_w[s], j * 16 + 16 * 9)
                    for m in range(4):
                        pe.wait_ge(gate_evac, j * 8 + (4 * s + m + 1))
                        for k in range(KT):
                            mm = pe.matmul(PS[4 * s + m][:, 0:TOKENS], W[s][:, k, P * m:P * (m + 1)], HT[:, k, :],
                                           start=(k == 0), stop=(k == KT - 1))
                        mm.then_inc(gate_mm, 1)
            pe.wait_ge(gate_evac, 8 + 16)
            for n in range(18):
                if n >= 4:
                    pe.wait_ge(turn2_evac, n - 3)
                t, q = (n // 4, n % 4) if n < 12 else ((n - 12) // 2, n % 2)
                r = ROWS[t]
                pe.wait_ge(y_scaled, t + 1)
                src = XS if n < 12 else O
                for m in range(4):
                    mm = pe.transpose(quads(PS[n % 4])[:, m, 0:r], src[0:r, t, P * (4 * q + m):P * (4 * q + m + 1)],
                                      const("ident", r, r))
                mm.then_inc(turn2_mm, 1)
            pe.wait_ge(turn2_evac, 18)
            for s in range(2):
                pe.wait_ge(s_w[s], 16 * 11)
                for m in range(4):
                    for k in range(KT):
                        mm = pe.matmul(PS[4 * s + m][:, 0:TOKENS], W[s][:, k, P * m:P * (m + 1)], OT[:, k, :],
                                       start=(k == 0), stop=(k == KT - 1))
                    mm.then_inc(oa_mm, 1)
            pe.wait_ge(oa_evac, 8)
            with pe.Fori(0, 2) as j:
                for s in range(2):
                    pe.wait_ge(s_w[s], j * 16 + 16 * 12)
                    for m in range(2):
                        pe.wait_ge(ob_evac, j * 4 + (2 * s + m + 1))
                        for k in range(16):
                            mm = pe.matmul(PS[4 * s + m][:, 0:TOKENS], W16[s][:, k, P * m:P * (m + 1)], YT[:, k, :],
                                           start=(k == 0), stop=(k == 15))
                        mm.then_inc(ob_mm, 1)
            pe.wait_ge(ob_evac, 4 + 8)
            for s in range(2):
                pe.wait_ge(s_w[s], 16 * 14)
                for t in range(TILES):
                    r = ROWS[t]
                    for k in range(KT):
                        mm = pe.matmul(PS[4 * s + t][0:r, :], MERGED[:, k, TOK0[t]:TOK0[t] + r], W[s][:, k, :],
                                       start=(k == 0), stop=(k == KT - 1))
                    mm.then_inc(out_mm, 1)

        def scalar_mixer(act, chain):
            summed = 0

            def square_sum(src, r, col, sink):
                nonlocal summed
                if summed:
                    act.wait_ge(squares, summed)
                summed += 1
                act.activation(sink, src, ACT.Square, accum_out=RMS[0:r, col:col + 1]).then_inc(squares, 1)

            act.sem_inc(raw_ready, 8)
            act.sem_inc(qkv_evac, 6)
            act.sem_inc(gate_evac, 8)
            act.wait_ge(rms_init, 1)
            for t in range(TILES):
                act.wait_ge(s_x, 32)
                r = ROWS[t]
                square_sum(X[0:r, t, :], r, t, SQ[0:r, :])
            act.wait_ge(variance, 1)
            act.activation(RMS[:, 0:3], RMS[:, 0:3], ACT.Sqrt).then_inc(deviation, 1)
            with act.Fori(0, 3) as j:
                for s in range(2):
                    for m in range(4):
                        raw = RAWB[:, s, m, :]
                        act.wait_ge(xbc_mm, j * 8 + (4 * s + m + 1))
                        act.wait_ge(conv_done, j * 8 + (4 * s + m + 1))
                        act.wait_ge(tails_done, j * 8 + (4 * s + m + 1))
                        act.activation(raw[:, TAPS - 1:PROMPT_RAW], PS[4 * s + m][:, 0:SEQ], ACT.Copy)
                        act.activation(
                            raw[:, PROMPT_RAW + 1:RAW].rearrange("p (b i) -> p b i", b=DEC_BATCH)[:, :, TAPS - 1:],
                            PS[4 * s + m][:, SAMPLE].rearrange("p (b i) -> p b i", b=DEC_BATCH),
                            ACT.Copy).then_inc(raw_ready, 1)
            with act.Fori(0, 2) as j:
                for s in range(2):
                    for t in range(TILES):
                        r = ROWS[t]
                        act.wait_ge(qkv_mm, j * 6 + (3 * s + t + 1))
                        act.activation(QKV[0:r, t, bass.ds(j * (2 * CH) + CH * s, CH)], PS[4 * s + t][0:r, :],
                                       ACT.Copy).then_inc(qkv_evac, 1)
            act.wait_ge(conv_done, 8 + 24)
            for half in range(2):
                v = XBC[:, 12 * half:12 * half + 12, :]
                act.activation(v, v, ACT.Silu).then_inc(silu_xbc, 1)
            act.wait_ge(s_par, 32)
            act.activation(NA, a_log, ACT.Exp).then_inc(na_ready, 1)
            act.wait_ge(dt_arg, 1)
            act.activation(ECUM, TOEND, ACT.Exp).then_inc(dt_exp, 1)
            act.wait_ge(dt_w, 1)
            act.activation(LNW, CUM, ACT.Ln).then_inc(dt_ln, 1)
            for n in range(21):
                act.wait_ge(turn_mm, n + 1)
                bank = PS[4 + n % 4]
                if n < 12:
                    t, q = n // 4, n % 4
                    dst, src = XS[0:ROWS[t], t, CH * q:CH * (q + 1)], bank[0:ROWS[t], :]
                elif n < 15:
                    t = n - 12
                    dst, src = BTOK[0:ROWS[t], t, :], bank[0:ROWS[t], :]
                else:
                    t, half = (n - 15) // 2, (n - 15) % 2
                    dst = QKT[:, 4 * half:4 * half + 4, TOK0[t]:TOK0[t] + ROWS[t]]
                    src = quads(bank)[:, :, 0:ROWS[t]]
                act.activation(dst, src, ACT.Copy).then_inc(turn_evac, 1)
                if n == 14:
                    act.wait_ge(cum_read, 1)
                    for lo, hi, r in ((0, 2, P), (2, 3, NS)):
                        act.activation(ECUM[0:r, lo:hi, :], CUM[0:r, lo:hi, :], ACT.Exp)
                        act.activation(TOEND[0:r, lo:hi, :], TOEND[0:r, lo:hi, :], ACT.Exp)
                    act.activation(DEC_P, DEC_P, ACT.Exp)
                    act.activation(DEC_S, DEC_S, ACT.Exp).then_inc(cum_exp, 1)
            for u, (t, g) in enumerate(UNITS):
                r = ROWS[t]
                for half in range(2):
                    act.wait_ge(seg_sub, 2 * u + half + 1)
                    v = SEG[0:r, u % 2, 4 * half:4 * half + 4, 0:r]
                    act.activation(v, v, ACT.Exp).then_inc(seg_exp, 1)
            for t in range(TILES):
                r = ROWS[t]
                if t == 0:
                    act.wait_ge(sample_y, 1)
                for h in range(RET_HEADS):
                    square_sum(O[0:r, t, RET_DV * h:RET_DV * (h + 1)], r, 4 + 4 * t + h, SQ[0:r, 0:RET_DV])
            act.wait_ge(variance, 2)
            act.activation(RMS[:, 4:16], RMS[:, 4:16], ACT.Sqrt).then_inc(deviation, 1)
            for s in range(2):
                for t in range(TILES):
                    i, r = 3 * s + t, ROWS[t]
                    act.wait_ge(g_mm, i + 1)
                    act.wait_ge(sil_used, i + 1)
                    act.activation(SIL[i % 2][0:r, :], PS[4 * s + t][0:r, :], ACT.Silu).then_inc(sil_ready, 1)
            with act.Fori(0, 2) as j:
                for s in range(2):
                    for t in range(TILES):
                        i, r = 3 * s + t, ROWS[t]
                        act.wait_ge(z_mm, j * 6 + (i + 1))
                        act.wait_ge(sil_used, j * 6 + (6 + i + 1))
                        act.activation(SIL[i % 2][0:r, :], PS[4 * s + t][0:r, :], ACT.Silu).then_inc(sil_ready, 1)
            act.wait_ge(sil_used, 2 + 18)
            for t in range(TILES):
                r = ROWS[t]
                for g in range(GROUPS):
                    square_sum(XS[0:r, t, GW * g:GW * (g + 1)], r, 16 + 4 * t + g, SQ[0:r, 0:GW])
            act.wait_ge(variance, 3)
            act.activation(RMS[:, 16:28], RMS[:, 16:28], ACT.Sqrt).then_inc(deviation, 1)
            with act.Fori(0, 2) as j:
                for s in range(2):
                    for m in range(4):
                        act.wait_ge(gate_mm, j * 8 + (4 * s + m + 1))
                        act.activation(SG[:, bass.ds(j * 8 + (4 * s + m), 1), :].squeeze(1),
                                       PS[4 * s + m][:, 0:TOKENS], ACT.Sigmoid).then_inc(gate_evac, 1)

        def rms_of(dve, chain, lo, hi, width, nth, n_squares):
            v = RMS[:, lo:hi]
            dve.wait_ge(squares, n_squares)
            dve.tensor_scalar(v, v, 1.0 / width, EPS, ALU.mult, ALU.add).then_inc(variance, 1)
            dve.wait_ge(deviation, nth)
            chain.link(dve.reciprocal(v, v))

        def vector_mixer(dve, chain):
            dve.sem_inc(conv_done, 8)
            dve.sem_inc(upd_evac, 2)
            dve.sem_inc(sil_used, 2)
            dve.sem_inc(ob_evac, 4)
            dve.memset(RMS, 1.0).then_inc(rms_init, 1)
            dve.memset(ZERO, 0.0).then_inc(zero_ready, 1)
            chain.link(dve.memset(DTW, 0.0))
            dve.wait_ge(rms_init, 1)
            rms_of(dve, chain, 0, 3, D_MODEL, 1, 3)
            for t in range(TILES):
                r = ROWS[t]
                dve.tensor_scalar(H[0:r, t, :], X[0:r, t, :], RMS[0:r, t:t + 1], None,
                                  ALU.mult).then_inc(h_ready, 1)
            dve.wait_ge(s_par, 32)
            for n in range(6):
                t, k0 = n // 2, 4 * (n % 2)
                r = ROWS[t]
                dve.wait_ge(h_turned, n + 1)
                dve.tensor_tensor(HT[:, k0:k0 + 4, TOK0[t]:TOK0[t] + r], quads(PS[n])[:, :, 0:r],
                                  heads(norm_mix[:, k0:k0 + 4], 4, r), ALU.mult).then_inc(ht_ready, 1)
            with chain.fori(3, 24) as j:
                for s in range(2):
                    for m in range(4):
                        raw = RAWB[:, s, m, :]
                        raw_s = raw[:, PROMPT_RAW + 1:RAW].rearrange("p (b i) -> p b i", b=DEC_BATCH)
                        mt = bass.ds(j * 8 + (4 * s + m), 1)
                        out = XBC[:, mt, :].squeeze(1)
                        out_s = out[:, SAMPLE].rearrange("p (b i) -> p b i", b=DEC_BATCH)
                        w = conv_w[:, mt, :].squeeze(1)
                        dve.wait_ge(raw_ready, j * 8 + (4 * s + m + 9))
                        dve.wait_ge(pads_ready, j * 8 + (4 * s + m + 1))
                        for i in range(TAPS):
                            for o_, x_ in ((out[:, 0:SEQ], raw[:, i:i + SEQ]), (out_s, raw_s[:, :, i:i + DEC_SEQ])):
                                if i == 0:
                                    ins = dve.tensor_scalar(o_, x_, w[:, 0:1], conv_b[:, mt], ALU.mult, ALU.add)
                                else:
                                    ins = dve.scalar_tensor_tensor(o_, x_, w[:, i:i + 1], o_, ALU.mult, ALU.add)
                            if i < TAPS - 1:
                                chain.link(ins)
                            else:
                                ins.then_inc(conv_done, 1)
            dve.wait_ge(dt_mm, 1)
            for t in range(TILES):
                r = ROWS[t]
                ins = dve.tensor_tensor(DT[0:r, t, :], PS[3][0:r, 32 * t:32 * t + 32], dt_bias[0:r], ALU.add)
            chain.link(ins)
            dve.scalar_tensor_tensor(TOEND, DT, -1.0, DT, ALU.mult, ALU.min).then_inc(dt_arg, 1)
            dve.wait_ge(dt_exp, 1)
            dve.tensor_scalar(CUM, ECUM, 1.0, None, ALU.add).then_inc(dt_w, 1)
            dve.wait_ge(dt_w, 1)
            chain.link(dve.tensor_scalar(TOEND, CUM, -1.0, None, ALU.add))
            chain.link(dve.tensor_tensor(TOEND, ECUM, TOEND, ALU.subtract))
            chain.link(dve.reciprocal(ECUM, CUM))
            chain.link(dve.tensor_tensor(TOEND, TOEND, ECUM, ALU.mult))
            dve.wait_ge(dt_ln, 1)
            chain.link(dve.tensor_tensor(LNW, LNW, TOEND, ALU.add))
            chain.link(dve.scalar_tensor_tensor(DT, DT, 0.0, LNW, ALU.max, ALU.add))
            dve.wait_ge(na_ready, 1)
            dve.scalar_tensor_tensor(DTA, DT, -1.0, NA.unsqueeze(1).to_broadcast([P, TILES, 32]),
                                     ALU.mult, ALU.mult).then_inc(dta_ready, 1)
            dve.wait_ge(qkv_evac, 6 + 6)
            for t in range(TILES):
                r = ROWS[t]
                qk = QKV[0:r, t, 0:1024].rearrange("p (h e n) -> p h e n", h=8, e=2)
                lo, hi = qk[:, :, 0, :], qk[:, :, 1, :]
                cos, sin = (const(n, 64, r, 64 * t).unsqueeze(1).to_broadcast([r, 8, 64]) for n in ("cos", "sin"))
                parts = [ROT[0:r, a, :].rearrange("p (h n) -> p h n", h=8) for a in range(4)]
                for out, a, b in zip(parts, (lo, hi, lo, hi), (cos, sin, sin, cos)):
                    ins = dve.tensor_tensor(out, a, b, ALU.mult)
                chain.link(ins)
                dve.tensor_tensor(lo, parts[0], parts[1], ALU.subtract)
                ins = dve.tensor_tensor(hi, parts[2], parts[3], ALU.add)
                ins.then_inc(rotated, 1)
                dve.wait_ge(rotated, t + 1)
            dve.wait_ge(cum_mm, 1)
            bank = PS[3]
            for lo, hi, r in ((0, 2, P), (2, 3, NS)):
                ins = dve.tensor_copy(CUM[0:r, lo:hi, :],
                                      bank[0:r, 32 * lo:32 * hi].rearrange("p (t h) -> p t h", h=32))
            chain.link(ins)
            for lo, hi, r in ((0, 2, P), (2, 3, NS)):
                dve.tensor_tensor(TOEND[0:r, lo:hi, :],
                                  bank[0:r, 96 + 32 * lo:96 + 32 * hi].rearrange("p (t h) -> p t h", h=32),
                                  CUM[0:r, lo:hi, :], ALU.subtract)
            dve.tensor_copy(DEC_P, bank[:, 128:160])
            dve.tensor_copy(DEC_S, bank[:, 192:448].rearrange("p (b h) -> p b h", h=32)).then_inc(cum_read, 1)
            dve.wait_ge(cum_exp, 1)
            for lo, hi, r in ((0, 2, P), (2, 3, NS)):
                ins = dve.tensor_tensor(TOEND[0:r, lo:hi, :], TOEND[0:r, lo:hi, :], DT[0:r, lo:hi, :], ALU.mult)
            ins.then_inc(toend_ready, 1)
            dve.wait_ge(turn_evac, 21)
            dve.tensor_tensor(QTD, QKT[:, 0:RET_HEADS, P:TOKENS],
                              const("q_decay", 768).rearrange("p (h n) -> p h n", h=RET_HEADS),
                              ALU.mult).then_inc(qtd_ready, 1)

            def sub(u):
                t, g = UNITS[u]
                r = ROWS[t]
                mask = const("mask_s" if t == 2 else "mask", r, r)
                if u >= 2:
                    dve.wait_ge(back_mm, u - 1)
                for h in range(HPG):
                    if h % 4 == 0:
                        dve.wait_ge(seg_mm, 2 * u + h // 4 + 1)
                    ins = dve.scalar_tensor_tensor(
                        SEG[0:r, u % 2, h, 0:r], quads(seg_bank(u, h // 4))[0:r, h % 4, 0:r],
                        CUM[0:r, t, HPG * g + h:HPG * g + h + 1], mask, ALU.subtract, ALU.min)
                    if h % 4 == 3:
                        ins.then_inc(seg_sub, 1)

            def weigh(u):
                t, g = UNITS[u]
                r = ROWS[t]
                dve.wait_ge(seg_exp, 2 * u + 2)
                v = SEG[0:r, u % 2, :, 0:r]
                cb = PS[4][0:r, P * (u % 2):P * (u % 2) + r]
                dve.tensor_tensor(v, v, cb.unsqueeze(1).to_broadcast([r, HPG, r]), ALU.mult).then_inc(wts_ready, 1)

            def spread(ap):
                return heads(ap, HPG, HEADDIM)

            def by_head(ap):
                return ap.rearrange("p (h n) -> p h n", h=HPG)

            def take(u):
                t, g = UNITS[u]
                r = ROWS[t]
                cols = slice(GW * g, GW * (g + 1))
                dve.wait_ge(back_mm, u + 1)
                if t == 2:
                    dve.tensor_tensor(XS[0:r, t, cols], XS[0:r, t, cols], PS[5][0:r, :], ALU.add).then_inc(y_evac, 1)
                    return
                chain.link(dve.tensor_tensor(XS[0:r, t, cols], XS[0:r, t, cols], PS[5][0:r, :], ALU.add))
                if t == 1:
                    dve.tensor_tensor(by_head(TMP[0:r, :]), by_head(PS[6][0:r, :]),
                                      spread(ECUM[0:r, t, HPG * g:HPG * (g + 1)]), ALU.mult)
                    chain.link(dve.tensor_tensor(by_head(SSM_PR[:, cols]), by_head(SSM_PR[:, cols]),
                                                 spread(DEC_P[:, HPG * g:HPG * (g + 1)]), ALU.mult))
                    dve.tensor_tensor(XS[0:r, t, cols], XS[0:r, t, cols], TMP[0:r, :], ALU.add)
                    dve.tensor_tensor(SSM_PR[:, cols], SSM_PR[:, cols], PS[7][:, :], ALU.add).then_inc(y_evac, 1)
                else:
                    dve.tensor_copy(SSM_PR[:, cols], PS[7][:, :]).then_inc(y_evac, 1)

            sub(0)
            for u in range(len(UNITS)):
                if u + 1 < len(UNITS):
                    sub(u + 1)
                weigh(u)
                if u >= 1:
                    take(u - 1)
            take(len(UNITS) - 1)

            def decayed(t, bank):
                r = ROWS[t]
                dve.wait_ge(score_mm, t + 1)
                decay = const("decay_s" if t == 2 else "decay", RET_HEADS * r, r)
                dve.tensor_tensor(SM[0:r, :, 0:r], quads(bank)[0:r, :, 0:r],
                                  decay.rearrange("p (h n) -> p h n", h=RET_HEADS), ALU.mult).then_inc(score_ready, 1)

            def o_out(t, banks):
                r = ROWS[t]
                for e in range(2):
                    ins = dve.tensor_copy(O[0:r, t, CH * e:CH * (e + 1)], banks[e][0:r, :])
                return ins

            decayed(0, PS[0])
            dve.wait_ge(ret_mm, 1)
            o_out(0, (PS[1], PS[2])).then_inc(ret_evac, 1)
            decayed(1, PS[5])
            dve.wait_ge(ret_mm, 2)
            for e in range(2):
                ins = dve.tensor_copy(RET_PR[:, CH * e:CH * (e + 1)], PS[3 + e][:, :])
            ins.then_inc(ret_evac, 1)
            dve.wait_ge(ret_mm, 3)
            o_out(1, (PS[6], PS[7])).then_inc(ret_evac, 1)
            dve.wait_ge(ret_evac, 2)
            dve.wait_ge(ret_mm, 4)
            for h in range(RET_HEADS):
                cols = slice(RET_DV * h, RET_DV * (h + 1))
                ins = dve.scalar_tensor_tensor(RET_PR[:, cols], RET_PR[:, cols], RET_GAMMA[h] ** P,
                                               PS[3 + h // 2][:, RET_DV * (h % 2):RET_DV * (h % 2 + 1)],
                                               ALU.mult, ALU.add)
            ins.then_inc(ret_evac, 1)
            decayed(2, PS[5])

            with chain.fori(DEC_BATCH // 2, 2) as j:
                for p in range(2):
                    dve.wait_ge(cross_mm, j * 2 + (p + 1))
                    for g in range(GROUPS):
                        v = by_head(SSM_IN[p][:, GW * g:GW * (g + 1)])
                        dec = DEC_S[:, bass.ds(j * 2 + p, 1), HPG * g:HPG * (g + 1)].squeeze(1)
                        ins = dve.tensor_tensor(v, v, spread(dec), ALU.mult)
                    chain.link(ins)
                    for u in range(6):
                        bank = PS[6 + u % 2]
                        dve.wait_ge(upd_mm, j * 12 + (6 * p + u + 1))
                        if u < 4:
                            v = SSM_IN[p][:, GW * u:GW * (u + 1)]
                            ins = dve.tensor_tensor(v, v, bank[:, :], ALU.add)
                        else:
                            for e in range(2):
                                h = 2 * (u - 4) + e
                                v = RET_IN[p][:, RET_DV * h:RET_DV * (h + 1)]
                                ins = dve.scalar_tensor_tensor(v, v, RET_GAMMA[h] ** DEC_SEQ,
                                                               bank[:, RET_DV * e:RET_DV * (e + 1)],
                                                               ALU.mult, ALU.add)
                        ins.then_inc(upd_evac, 1)
            dve.wait_ge(closed, 1)
            for g in range(GROUPS):
                cols = slice(GW * g, GW * (g + 1))
                chain.link(dve.tensor_tensor(by_head(TMP[0:NS, :]), by_head(PS[2 + g][0:NS, :]),
                                             spread(ECUM[0:NS, 2, HPG * g:HPG * (g + 1)]), ALU.mult))
                chain.link(dve.tensor_tensor(XS[0:NS, 2, cols], XS[0:NS, 2, cols], TMP[0:NS, :], ALU.add))
            o_out(2, (PS[0], PS[1])).then_inc(sample_y, 1)

            rms_of(dve, chain, 4, 16, RET_DV, 2, 3 + 12)
            for s in range(2):
                for t in range(TILES):
                    i, r = 3 * s + t, ROWS[t]
                    dve.wait_ge(sil_ready, i + 1)
                    for e in range(2):
                        v = O[0:r, t, CH * s + RET_DV * e:CH * s + RET_DV * (e + 1)]
                        col = 4 + 4 * t + 2 * s + e
                        ins = dve.scalar_tensor_tensor(v, v, RMS[0:r, col:col + 1],
                                                       SIL[i % 2][0:r, RET_DV * e:RET_DV * (e + 1)],
                                                       ALU.mult, ALU.mult)
                    ins.then_inc(sil_used, 1)
            with dve.Fori(0, 2) as j:
                for s in range(2):
                    for t in range(TILES):
                        i, r = 3 * s + t, ROWS[t]
                        dve.wait_ge(sil_ready, j * 6 + (6 + i + 1))
                        v = XS[0:r, t, bass.ds(j * (2 * GW) + GW * s, GW)]
                        dve.tensor_tensor(v, v, SIL[i % 2][0:r, :], ALU.mult).then_inc(sil_used, 1)
            rms_of(dve, chain, 16, 28, GW, 3, 15 + 12)
            for t in range(TILES):
                r = ROWS[t]
                for g in range(GROUPS):
                    v = XS[0:r, t, GW * g:GW * (g + 1)]
                    ins = dve.tensor_scalar(v, v, RMS[0:r, 16 + 4 * t + g:17 + 4 * t + g], None, ALU.mult)
                ins.then_inc(y_scaled, 1)
            for n in range(18):
                t, q = (n // 4, n % 4) if n < 12 else ((n - 12) // 2, n % 2)
                r = ROWS[t]
                dve.wait_ge(turn2_mm, n + 1)
                dst, wt = (YT, ssm_norm) if n < 12 else (OT, ret_norm)
                dve.tensor_tensor(dst[:, 4 * q:4 * q + 4, TOK0[t]:TOK0[t] + r], quads(PS[n % 4])[:, :, 0:r],
                                  heads(wt[:, 4 * q:4 * q + 4], 4, r), ALU.mult).then_inc(turn2_evac, 1)
            for n in range(8):
                dve.wait_ge(oa_mm, n + 1)
                dve.tensor_tensor(SG[:, n, :], SG[:, n, :], PS[n][:, 0:TOKENS], ALU.mult).then_inc(oa_evac, 1)
            dve.wait_ge(oa_evac, 8)
            with chain.fori(2, 4) as j:
                for s in range(2):
                    for m in range(2):
                        i = 2 * s + m
                        dve.wait_ge(ob_mm, j * 4 + (i + 1))
                        a = SG[:, bass.ds(j * 4 + i, 1), :].squeeze(1)
                        b = SG[:, bass.ds(j * 4 + (8 + i), 1), :].squeeze(1)
                        chain.link(dve.tensor_tensor(b, b, PS[4 * s + m][:, 0:TOKENS], ALU.mult))
                        dve.tensor_tensor(MERGED[:, bass.ds(j * 4 + i, 1), :].squeeze(1), a, b,
                                          ALU.add).then_inc(ob_evac, 1)
            for s in range(2):
                for t in range(TILES):
                    r = ROWS[t]
                    dve.wait_ge(out_mm, 3 * s + t + 1)
                    v = X[0:r, t, CH * s:CH * (s + 1)]
                    dve.tensor_tensor(v, v, PS[4 * s + t][0:r, :], ALU.add).then_inc(x1_ready, 1)

        def pool_mixer(pool, chain):
            pool.sem_inc(tails_done, 8)
            pool.wait_ge(s_par, 32)
            pool.memset(RAWB[:, :, :, 0:TAPS - 1], 0.0)
            with pool.Fori(0, 3) as j:
                for s in range(2):
                    for m in range(4):
                        raw = RAWB[:, s, m, :]
                        raw_s = raw[:, PROMPT_RAW + 1:RAW].rearrange("p (b i) -> p b i", b=DEC_BATCH)
                        mt = bass.ds(j * 8 + (4 * s + m), 1)
                        pool.wait_ge(conv_done, j * 8 + (4 * s + m + 1))
                        pool.tensor_copy(raw_s[:, :, 0:TAPS - 1],
                                         conv_state[:, mt, :, :].squeeze(1)).then_inc(pads_ready, 1)
                        pool.wait_ge(raw_ready, j * 8 + (4 * s + m + 9))
                        pool.wait_ge(pads_ready, j * 8 + (4 * s + m + 1))
                        pool.tensor_copy(CONV_TAIL[:, mt, :].squeeze(1), raw[:, SEQ:SEQ + TAPS - 1])
                        pool.tensor_copy(CONV_TAIL_S[:, mt, :, :].squeeze(1),
                                         raw_s[:, :, DEC_SEQ:DEC_SEQ + TAPS - 1]).then_inc(tails_done, 1)
            pool.wait_ge(toend_ready, 1)
            for u, (t, g) in enumerate(UNITS):
                r = ROWS[t]
                cols = slice(GW * g, GW * (g + 1))
                hs = slice(HPG * g, HPG * (g + 1))
                if g == 0:
                    pool.wait_ge(turn_evac, 4 * t + 4)
                if u >= 4:
                    pool.wait_ge(back_mm, u - 3)

                def by_head(ap):
                    return ap.rearrange("p (h n) -> p h n", h=HPG)

                x = by_head(XS[0:r, t, cols])
                pool.tensor_tensor(by_head(XDT[0:r, cols]), x, heads(DT[0:r, t, hs], HPG, HEADDIM), ALU.mult)
                chain.link(pool.tensor_tensor(by_head(XEND[0:r, cols]), x, heads(TOEND[0:r, t, hs], HPG, HEADDIM),
                                              ALU.mult))
                pool.tensor_tensor(x, x, heads(d_skip[0:r, hs], HPG, HEADDIM), ALU.mult).then_inc(xdt_ready, 1)
            for t in range(TILES):
                r = ROWS[t]
                if t == 0:
                    pool.wait_ge(rotated, 3)
                    pool.wait_ge(turn_evac, 21)
                else:
                    pool.wait_ge(ret_mm, 2 * t)
                pool.tensor_tensor(KDEC[0:r, :].rearrange("p (h n) -> p h n", h=RET_HEADS),
                                   QKV[0:r, t, 512:1024].rearrange("p (h n) -> p h n", h=RET_HEADS),
                                   heads(const("k_decay_s" if t == 2 else "k_decay", RET_HEADS, r), RET_HEADS, P),
                                   ALU.mult).then_inc(kdec_ready, 1)
            pool.wait_ge(kdec_ready, 3)
            pool.wait_ge(seg_exp, 24)
            pool.wait_ge(back_mm, 12)
            for j in range(DEC_BATCH // 2):
                for p in range(2):
                    b = 2 * j + p
                    if b >= 2:
                        pool.wait_ge(upd_mm, 6 * (b - 1))
                    cols = const("seq_cols", NS, P, NS * b).unsqueeze(1).to_broadcast([P, 4, NS])
                    row = const("seq_rows", 1, NS, b).to_broadcast([NS, 512])
                    pool.tensor_tensor(CTM[p], XBC[:, 20:24, SAMPLE], cols, ALU.mult)
                    pool.tensor_tensor(QTM[p], QTD[:, :, P:], cols, ALU.mult)
                    pool.tensor_tensor(BM[p], BTOK[0:NS, 2, :], row, ALU.mult)
                    pool.tensor_tensor(KM[p], KDEC[0:NS, :], row, ALU.mult).then_inc(masks_ready, 1)

        WA = region(0, 8192).rearrange("p (k e n) -> p k e n", k=KT, e=2)
        WB = region(8192, 8192).rearrange("p (k e n) -> p k e n", k=KT, e=2)
        WD = region(16384, 8192).rearrange("p (k n) -> p k n", k=KT)
        H2 = region(16384, 3072).rearrange("p (t n) -> p t n", t=TILES)
        H2T = region(19456, 2560).rearrange("p (k n) -> p k n", k=KT)
        CMP = region(22016, BLOCK_COLS * N_EXPERTS).rearrange("p (b e) -> p b e", e=N_EXPERTS)
        XG = region(24576, 1024)
        XTE = region(25600, 1024).rearrange("p (k n) -> p k n", k=KT)
        ACTB = region(26624, 1024)
        ACTT = region(27648, 1024).rearrange("p (k n) -> p k n", k=KT)
        YB = region(28672, 1024)
        GLU = region(29696, 1024).rearrange("p (c n) -> p c n", c=2)
        LIN = region(30720, 1024).rearrange("p (c n) -> p c n", c=2)
        SILU = region(31744, 1024).rearrange("p (c n) -> p c n", c=2)
        SELB = region(32768, 64).bitcast(BF16)
        NF = region(36096, 1024)
        BIAS = region(37120, 1536).bitcast(BF16)
        BIAS_F32 = region(24576, 3072)
        YS = region(0, 12288).rearrange("p (t n) -> p t n", t=TILES)
        OUT = region(12288, 3072).rearrange("p (t n) -> p t n", t=TILES)
        SQ_END = region(16384, 1024)

        o = 0

        def temp(n):
            nonlocal o
            o += n
            assert o <= 4608
            return TEMPS[:, o - n:o]

        def tiles(ap, n):
            return ap.rearrange("p (t n) -> p t n", n=n)

        LOG = tiles(temp(96), 32)
        TOP8 = tiles(temp(24), 8)
        IDX8 = tiles(temp(24).bitcast(U32), 8)
        IDX8F = tiles(temp(24), 8)
        CHOSEN = temp(384).rearrange("p (t k e) -> p t k e", t=TILES, k=TOP_K)
        TAKEN = tiles(temp(96), 32)
        RANK = tiles(temp(96), 32)
        RANK_DIV = tiles(temp(96), 32)
        LANE = tiles(temp(96), 32)
        BLOCK = tiles(temp(96), 32)
        COUNT = temp(32)
        BLOCKS_OF = temp(32)
        BLOCKS_TO = temp(32)
        FIRST_BLOCK = temp(32)
        PICKED = temp(384).rearrange("p (t k e) -> p t k e", t=TILES, k=TOP_K)
        LANE_K = tiles(temp(12), 4)
        BLOCK_K = tiles(temp(12), 4)
        GATE = tiles(temp(12), 4)
        GSUM = temp(3)
        IN_LANE = temp(1536).rearrange("p (t k n) -> p t k n", t=TILES, k=TOP_K)
        IN_BLOCK = temp(12 * BLOCK_COLS).rearrange("p (t k n) -> p t k n", t=TILES, k=TOP_K)
        EXPERT_F = temp(BLOCK_COLS)
        EXPERT = temp(BLOCK_COLS).bitcast(I32)
        N_BLOCKS = temp(1).bitcast(I32)
        SELECT = temp(BLOCK_COLS + 1).bitcast(BF16)
        EMPTY = temp(BLOCK_COLS)
        ASSIGN = temp(BLOCK_COLS).bitcast(I32)
        TOKEN = temp(BLOCK_COLS).bitcast(I32)
        GATHER_AT = temp(1).bitcast(I32)
        SCATTER_AT = temp(1).bitcast(I32)

        h2_dram = nc.dram_tensor("normalized_rows", (TOKENS, D_MODEL), F32).ap()
        ys_dram = nc.dram_tensor("assignment_rows", (TOKENS * TOP_K, D_MODEL), F32).ap()

        s_bias, s_nf, s_h2, s_ys = sem("biases_in"), sem("norm_final_in"), sem("h2_out"), sem("rows_in")
        s_wa, s_wb, s_wd = sem("weights_a_in"), sem("weights_b_in"), sem("weights_down_in")
        gathered, scattered, s_y = sem("gathered"), sem("scattered"), sem("y_out_done")
        bias_ready, h2_ready, turn3_mm, h2t_ready, logits_mm = (
            sem("bias_ready"), sem("h2_ready"), sem("turn3_mm"), sem("h2t_ready"), sem("logits_mm"))
        taken_ready, rank_mm, places_ready, lists_mm, lists_ready = (
            sem("taken_ready"), sem("rank_mm"), sem("places_ready"), sem("lists_mm"), sem("lists_ready"))
        gate_arg, gate_exp = sem("gate_arg"), sem("gate_exp")
        a_mm, b_mm, y_mm, act_turned, x_turned = (
            sem("a_mm"), sem("b_mm"), sem("y_mm"), sem("act_turned"), sem("x_turned"))
        x_ready, glu_ready, silu_ready, act_ready, actt_ready = (
            sem("x_ready"), sem("glu_ready"), sem("silu_ready"), sem("act_ready"), sem("actt_ready"))
        y_ready, y_stored, select_ready, end_sum = (
            sem("y_ready"), sem("y_stored"), sem("select_ready"), sem("end_sum"))
        out_ready = sem("out_ready")
        index_set = sem("index_set")
        XT_BANKS = (PS[5], PS[0])

        def sync_experts(sp):
            sp.wait_ge(turn2_evac, 18)
            for n in range(3):
                rows = slice(32 * n, 32 * n + 32)
                sp.dma_start(BIAS_F32[rows, 0:2 * D_FF], b_gate_up).then_inc(s_bias, 16)
                sp.dma_start(BIAS_F32[rows, 2 * D_FF:3 * D_FF], b_down).then_inc(s_bias, 16)
            sp.dma_start(NF, norm_final.to_broadcast([P, D_MODEL])).then_inc(s_nf, 16)
            sp.wait_ge(h2_ready, TILES)
            sp.dma_start(h2_dram[0:SEQ, :].rearrange("(t p) d -> p t d", p=P), H2[:, 0:2, :]).then_inc(s_h2, 16)
            sp.dma_start(h2_dram[SAMPLE, :], H2[0:NS, 2, :]).then_inc(s_h2, 16)

            def load_up(w, half, e, s):
                src = w_gate_up[bass.ds(e, 1), :, :].squeeze(0).rearrange("(k p) (u n) -> p k u n", p=P, u=2)
                for u in range(2):
                    sp.dma_start(w[:, :, u, :], src[:, :, u, CH * half:CH * (half + 1)]).then_inc(s, 16)

            def load_down(e):
                sp.dma_start(WD, w_down[bass.ds(e, 1), :, :].squeeze(0).rearrange("(k p) n -> p k n", p=P)
                             ).then_inc(s_wd, 16)

            sp.wait_ge(lists_ready, 1)
            n_blocks = sp.value_load(N_BLOCKS[0:1, 0:1], min_val=TOKENS * TOP_K // P, max_val=MAX_BLOCKS)
            e = sp.value_load(EXPERT[0:1, 0:1], min_val=0, max_val=N_EXPERTS - 1)
            load_up(WA, 0, e, s_wa)
            load_up(WB, 1, e, s_wb)
            sp.wait_ge(s_h2, 32)
            load_down(e)
            with sp.Fori(0, n_blocks - 1) as i:
                e = sp.value_load(EXPERT[0:1, bass.ds(i + 1, 1)], min_val=0, max_val=N_EXPERTS - 1)
                sp.wait_ge(a_mm, i * 2 + 2)
                load_up(WA, 0, e, s_wa)
                sp.wait_ge(b_mm, i * 2 + 2)
                load_up(WB, 1, e, s_wb)
                sp.wait_ge(y_mm, i * 2 + 2)
                load_down(e)
            sp.wait_ge(y_stored, n_blocks + 1)
            for t in range(TILES):
                r = ROWS[t]
                sp.dma_start(YS[0:r, t, :], ys_dram[TOK0[t] * TOP_K:(TOK0[t] + r) * TOP_K, :].rearrange(
                    "(p k) d -> p (k d)", k=TOP_K)).then_inc(s_ys, 16)
            for t in range(TILES):
                r = ROWS[t]
                sp.wait_ge(out_ready, t + 1)
                sp.dma_start(y_out[TOK0[t]:TOK0[t] + r, :], OUT[0:r, t, :]).then_inc(s_y, 16)
            sp.wait_ge(s_y, 16 * TILES)

        def tensor_experts(pe):
            ident = const("ident", P)
            for n in range(6):
                t, k0 = n // 2, 4 * (n % 2)
                r = ROWS[t]
                pe.wait_ge(h2_ready, t + 1)
                for k in range(4):
                    mm = pe.transpose(quads(PS[n])[:, k, 0:r], H2[0:r, t, P * (k0 + k):P * (k0 + k + 1)],
                                      const("ident", r, r))
                mm.then_inc(turn3_mm, 1)
            for t in range(TILES):
                r = ROWS[t]
                pe.wait_ge(h2t_ready, 6)
                for k in range(KT):
                    mm = pe.matmul(PS[5 + t][0:r, 0:32], H2T[:, k, TOK0[t]:TOK0[t] + r], WR[:, k, :],
                                   start=(k == 0), stop=(k == KT - 1))
                mm.then_inc(logits_mm, 1)
            pe.wait_ge(taken_ready, 1)
            for t in range(TILES):
                r = ROWS[t]
                for s in range(t + 1):
                    lhs = const("before", r, r) if s == t else const("ones", r, P)
                    pe.matmul(PS[7][0:r, 32 * t:32 * t + 32], lhs, TAKEN[0:ROWS[s], s, :],
                              start=(s == 0), stop=(s == t))
            for s in range(TILES):
                mm = pe.matmul(PS[7][:, 96:128], const("ones", P, ROWS[s]), TAKEN[0:ROWS[s], s, :],
                               start=(s == 0), stop=(s == TILES - 1))
            mm.then_inc(rank_mm, 1)
            pe.wait_ge(places_ready, 1)
            for t in range(TILES):
                r = ROWS[t]
                for k in range(TOP_K):
                    mm = pe.matmul(PS[0][:, 0:BLOCK_COLS], IN_LANE[0:r, t, k, :], IN_BLOCK[0:r, t, k, :],
                                   start=(t + k == 0), stop=(t == TILES - 1 and k == TOP_K - 1))
            mm.then_inc(lists_mm, 1)

            def turn_x():
                for e in range(2):
                    for k in range(4):
                        mm = pe.transpose(quads(XT_BANKS[e])[:, k, :], XG[:, P * (4 * e + k):P * (4 * e + k + 1)],
                                          ident)
                    mm.then_inc(x_turned, 1)

            def turn_act(c):
                for k in range(4):
                    mm = pe.transpose(quads(PS[4])[:, k, :], ACTB[:, P * (4 * c + k):P * (4 * c + k + 1)], ident)
                mm.then_inc(act_turned, 1)

            pe.wait_ge(lists_ready, 1)
            n_blocks = pe.value_load(N_BLOCKS[0:1, 0:1], min_val=TOKENS * TOP_K // P, max_val=MAX_BLOCKS)
            pe.wait_ge(bias_ready, 1)
            pe.wait_ge(gathered, 16)
            turn_x()
            with pe.Fori(0, n_blocks) as i:
                pe.wait_ge(select_ready, i + 1)
                pe.wait_ge(x_ready, i * 2 + 2)
                for half, w, s_in, done in ((0, WA, s_wa, a_mm), (1, WB, s_wb, b_mm)):
                    pe.wait_ge(s_in, i * 32 + 32)
                    for u in range(2):
                        bank = PS[2 * half + u]
                        at = D_FF * u + CH * half
                        pe.matmul(bank[:, :], SELB[0:96, :], BIAS[0:96, at:at + CH], start=True, stop=False)
                        for k in range(KT):
                            mm = pe.matmul(bank[:, :], XTE[:, k, :], w[:, k, u, :], start=False,
                                           stop=(k == KT - 1))
                        mm.then_inc(done, 1)
                pe.wait_ge(act_ready, i * 2 + 1)
                turn_act(0)
                pe.wait_ge(gathered, i * 16 + 32)
                turn_x()
                pe.wait_ge(s_wd, i * 16 + 16)
                pe.wait_ge(y_ready, i * 2 + 2)
                for c in range(2):
                    if c == 1:
                        pe.wait_ge(act_ready, i * 2 + 2)
                        turn_act(1)
                    pe.wait_ge(actt_ready, i * 2 + (c + 1))
                    for n in range(2):
                        bank, cols = PS[6 + n], slice(CH * n, CH * (n + 1))
                        if c == 0:
                            pe.matmul(bank[:, :], SELB[0:96, :], BIAS[0:96, 2 * D_FF + CH * n:2 * D_FF + CH * (n + 1)],
                                      start=True, stop=False)
                        for k in range(4 * c, 4 * c + 4):
                            mm = pe.matmul(bank[:, :], ACTT[:, k, :], WD[:, k, cols], start=False, stop=(k == KT - 1))
                        if c == 1:
                            mm.then_inc(y_mm, 1)

        def scalar_experts(act, chain):
            for t in range(TILES):
                r = ROWS[t]
                act.wait_ge(x1_ready, 3 + t + 1)
                act.wait_ge(squares, 27 + t)
                act.activation(SQ[0:r, :], X[0:r, t, :], ACT.Square,
                               accum_out=RMS[0:r, 28 + t:29 + t]).then_inc(squares, 1)
            act.wait_ge(variance, 4)
            act.activation(RMS[:, 28:31], RMS[:, 28:31], ACT.Sqrt).then_inc(deviation, 1)
            act.wait_ge(gate_arg, 1)
            act.activation(GATE, GATE, ACT.Exp).then_inc(gate_exp, 1)
            act.wait_ge(lists_ready, 1)
            n_blocks = act.value_load(N_BLOCKS[0:1, 0:1], min_val=TOKENS * TOP_K // P, max_val=MAX_BLOCKS)
            with act.Fori(0, n_blocks) as i:
                for c in range(2):
                    act.wait_ge(glu_ready, i * 2 + (c + 1))
                    act.activation(SILU[:, c, :], GLU[:, c, :], ACT.Silu, scale=ALPHA).then_inc(silu_ready, 1)
                    act.wait_ge(act_turned, i * 2 + (c + 1))
                    act.activation(ACTT[:, 4 * c:4 * c + 4, :], quads(PS[4]), ACT.Copy,
                                   scale=1.0 / ALPHA).then_inc(actt_ready, 1)
                act.wait_ge(y_mm, i * 2 + 1)
                act.wait_ge(y_stored, i + 1)
                act.activation(YB[:, 0:CH], PS[6][:, :], ACT.Copy).then_inc(y_ready, 1)
            for t in range(TILES):
                r = ROWS[t]
                act.wait_ge(end_sum, TOP_K * (t + 1))
                act.wait_ge(squares, 30 + t)
                act.activation(SQ_END[0:r, :], X[0:r, t, :], ACT.Square,
                               accum_out=RMS[0:r, 28 + t:29 + t]).then_inc(squares, 1)
                act.wait_ge(variance, 5 + t)
                act.activation(RMS[:, 28 + t:29 + t], RMS[:, 28 + t:29 + t], ACT.Sqrt).then_inc(deviation, 1)

        def vector_experts(dve, chain):
            dve.sem_inc(y_ready, 2)
            rms_of(dve, chain, 28, 31, D_MODEL, 4, 30)
            for t in range(TILES):
                r = ROWS[t]
                dve.tensor_scalar(H2[0:r, t, :], X[0:r, t, :], RMS[0:r, 28 + t:29 + t], None,
                                  ALU.mult).then_inc(h2_ready, 1)
            for n in range(6):
                t, k0 = n // 2, 4 * (n % 2)
                r = ROWS[t]
                dve.wait_ge(turn3_mm, n + 1)
                dve.tensor_tensor(H2T[:, k0:k0 + 4, TOK0[t]:TOK0[t] + r], quads(PS[n])[:, :, 0:r],
                                  heads(norm_ffn[:, k0:k0 + 4], 4, r), ALU.mult).then_inc(h2t_ready, 1)
            dve.memset(RANK, 0.0)
            chain.link(dve.memset(CHOSEN, 0.0))
            for t in range(TILES):
                r = ROWS[t]
                dve.wait_ge(logits_mm, t + 1)
                chain.link(dve.tensor_tensor(LOG[0:r, t, :], PS[5 + t][0:r, 0:32], b_router[0:r], ALU.add))
                chain.link(dve.max(TOP8[0:r, t, :], LOG[0:r, t, :]))
                chain.link(dve.max_index(IDX8[0:r, t, :], TOP8[0:r, t, :], LOG[0:r, t, :]))
                chain.link(dve.tensor_copy(IDX8F[0:r, t, :], IDX8[0:r, t, :]))
                chain.link(dve.tensor_tensor(
                    CHOSEN[0:r, t, :, :], const("experts", 32, r).unsqueeze(1).to_broadcast([r, TOP_K, N_EXPERTS]),
                    heads(IDX8F[0:r, t, 0:TOP_K], TOP_K, N_EXPERTS), ALU.is_equal))
                ins = dve.tensor_reduce(TAKEN[0:r, t, :], CHOSEN[0:r, t, :, :].rearrange("p k e -> p e k"),
                                        AX.X, ALU.add)
                if t < TILES - 1:
                    chain.link(ins)
                else:
                    ins.then_inc(taken_ready, 1)
            for t in range(TILES):
                r = ROWS[t]
                ins = dve.tensor_scalar(GATE[0:r, t, :], TOP8[0:r, t, 0:TOP_K], TOP8[0:r, t, 0:1], None,
                                        ALU.subtract)
            dve.tensor_scalar(GATE[NS:P, 2, :], RMS[NS:P, 0:TOP_K], 0.0, None, ALU.mult).then_inc(gate_arg, 1)
            dve.wait_ge(rank_mm, 1)
            dve.tensor_copy(RANK[:, 0:2, :], PS[7][:, 0:64].rearrange("p (t e) -> p t e", t=2))
            dve.tensor_copy(RANK[0:NS, 2, :], PS[7][0:NS, 64:96])
            chain.link(dve.tensor_copy(COUNT, PS[7][:, 96:128]))
            dve.tensor_scalar(BLOCKS_OF, COUNT, 0.0, None, ALU.is_gt)
            chain.link(dve.tensor_scalar(RANK_DIV, RANK, float(P), None, ALU.is_ge))
            for n in range(1, -(-TOKENS // P)):
                if n > 1:
                    dve.scalar_tensor_tensor(RANK_DIV, RANK, float(P * n), RANK_DIV, ALU.is_ge, ALU.add)
                chain.link(dve.scalar_tensor_tensor(BLOCKS_OF, COUNT, float(P * n), BLOCKS_OF, ALU.is_gt, ALU.add))
            chain.link(dve.tensor_tensor_scan(BLOCKS_TO, const("ones", N_EXPERTS), BLOCKS_OF, 0.0,
                                              ALU.mult, ALU.add))
            chain.link(dve.tensor_tensor(FIRST_BLOCK, BLOCKS_TO, BLOCKS_OF, ALU.subtract))
            dve.scalar_tensor_tensor(LANE, RANK_DIV, -float(P), RANK, ALU.mult, ALU.add)
            chain.link(dve.tensor_tensor(BLOCK, RANK_DIV, FIRST_BLOCK.unsqueeze(1).to_broadcast([P, TILES, 32]),
                                         ALU.add))
            for src, dst in ((LANE, LANE_K), (BLOCK, BLOCK_K)):
                for t in range(TILES):
                    ins = dve.tensor_tensor(PICKED[:, t, :, :], CHOSEN[:, t, :, :],
                                            src[:, t, :].unsqueeze(1).to_broadcast([P, TOP_K, N_EXPERTS]), ALU.mult)
                chain.link(ins)
                chain.link(dve.tensor_reduce(dst, PICKED, AX.X, ALU.add))
            for t in range(TILES):
                dve.tensor_tensor(IN_LANE[:, t, :, :], const("lanes", P).unsqueeze(1).to_broadcast([P, TOP_K, P]),
                                  heads(LANE_K[:, t, :], TOP_K, P), ALU.is_equal)
                ins = dve.tensor_tensor(IN_BLOCK[:, t, :, :],
                                        const("blocks", BLOCK_COLS).unsqueeze(1).to_broadcast([P, TOP_K, BLOCK_COLS]),
                                        heads(BLOCK_K[:, t, :], TOP_K, BLOCK_COLS), ALU.is_equal)
            chain.link(ins)
            for t in range(TILES):
                ins = dve.tensor_tensor(IN_BLOCK[:, t, :, :], IN_BLOCK[:, t, :, :],
                                        heads(const("assign", TOP_K, P, TOP_K * t), TOP_K, BLOCK_COLS), ALU.mult)
            ins.then_inc(places_ready, 1)
            chain.link(dve.tensor_tensor(CMP, BLOCKS_TO.unsqueeze(1).to_broadcast([P, BLOCK_COLS, N_EXPERTS]),
                                         heads(const("blocks", BLOCK_COLS), BLOCK_COLS, N_EXPERTS), ALU.is_le))
            chain.link(dve.tensor_reduce(EXPERT_F, CMP, AX.X, ALU.add))
            dve.tensor_scalar(SELECT[0:96, 0:BLOCK_COLS], EXPERT_F[0:96, :], const("mod32", 1, 96), None,
                              ALU.is_equal)
            dve.tensor_scalar(EXPERT[0:1, :], EXPERT_F[0:1, :], float(N_EXPERTS - 1), None, ALU.min)
            dve.tensor_copy(N_BLOCKS[0:1, :], BLOCKS_TO[0:1, N_EXPERTS - 1:N_EXPERTS])
            dve.wait_ge(lists_mm, 1)
            chain.link(dve.tensor_scalar(EMPTY, PS[0][:, 0:BLOCK_COLS], 0.0, NOWHERE, ALU.is_equal, ALU.mult))
            chain.link(dve.scalar_tensor_tensor(ASSIGN, PS[0][:, 0:BLOCK_COLS], -1.0, EMPTY, ALU.add, ALU.add))
            dve.tensor_scalar(TOKEN, ASSIGN, 2, None, ALU.logical_shift_right).then_inc(lists_ready, 1)
            dve.wait_ge(gate_exp, 1)
            chain.link(dve.tensor_reduce(GSUM, GATE, AX.X, ALU.add))
            chain.link(dve.reciprocal(GSUM, GSUM))
            chain.link(dve.tensor_tensor(GATE, GATE, heads(GSUM, TILES, TOP_K), ALU.mult))

            def x_out(done):
                for e in range(2):
                    dve.wait_ge(x_turned, done + (e + 1))
                    dve.tensor_tensor(XTE[:, 4 * e:4 * e + 4, :], quads(XT_BANKS[e]),
                                      heads(norm_ffn[:, 4 * e:4 * e + 4], 4, P), ALU.mult).then_inc(x_ready, 1)

            dve.wait_ge(lists_ready, 1)
            n_blocks = dve.value_load(N_BLOCKS[0:1, 0:1], min_val=TOKENS * TOP_K // P, max_val=MAX_BLOCKS)
            dve.tensor_copy(SELB[0:96, :], SELECT[0:96, 0:1].to_broadcast([96, P])).then_inc(select_ready, 1)
            x_out(0)
            with chain.fori(n_blocks, 2) as i:
                for c, mms in ((0, a_mm), (1, b_mm)):
                    dve.wait_ge(mms, i * 2 + 1)
                    dve.tensor_scalar(GLU[:, c, :], PS[2 * c][:, :], LIMIT, None, ALU.min).then_inc(glu_ready, 1)
                    dve.wait_ge(mms, i * 2 + 2)
                    chain.link(dve.tensor_scalar(LIN[:, c, :], PS[2 * c + 1][:, :], LIMIT, -LIMIT,
                                                 ALU.min, ALU.max))
                    dve.wait_ge(silu_ready, i * 2 + (c + 1))
                    dve.scalar_tensor_tensor(ACTB[:, CH * c:CH * (c + 1)], LIN[:, c, :], 1.0, SILU[:, c, :],
                                             ALU.add, ALU.mult).then_inc(act_ready, 1)
                x_out(i * 2 + 2)
                dve.wait_ge(y_mm, i * 2 + 2)
                dve.tensor_copy(SELB[0:96, :],
                                SELECT[0:96, bass.ds(i + 1, 1)].to_broadcast([96, P])).then_inc(select_ready, 1)
                dve.wait_ge(y_stored, i + 1)
                dve.tensor_copy(YB[:, CH:2 * CH], PS[7][:, :]).then_inc(y_ready, 1)
            dve.wait_ge(s_nf, 16)
            for t in range(TILES):
                r = ROWS[t]
                dve.wait_ge(s_ys, 16 * TILES)
                for k in range(TOP_K):
                    dve.scalar_tensor_tensor(X[0:r, t, :], YS[0:r, t, D_MODEL * k:D_MODEL * (k + 1)],
                                             GATE[0:r, t, k:k + 1], X[0:r, t, :],
                                             ALU.mult, ALU.add).then_inc(end_sum, 1)
                    dve.wait_ge(end_sum, TOP_K * t + k + 1)
                rms_of(dve, chain, 28 + t, 29 + t, D_MODEL, 5 + t, 31 + t)
                dve.scalar_tensor_tensor(OUT[0:r, t, :], X[0:r, t, :], RMS[0:r, 28 + t:29 + t], NF[0:r, :],
                                         ALU.mult, ALU.mult).then_inc(out_ready, 1)

        def pool_experts(pool, chain):
            pool.sem_inc(y_stored, 1)
            pool.wait_ge(s_bias, 96)
            parts = [slice(32 * n, 32 * n + 32) for n in range(3)]
            chain.link(pool.tensor_copy(BIAS[0:96, :], BIAS_F32[0:96, :]))
            for n in range(1, 3):
                for m in range(n, 3):
                    ins = pool.tensor_tensor(BIAS_F32[parts[m], :], BIAS_F32[parts[m], :], BIAS[parts[m], :],
                                             ALU.subtract)
                chain.link(ins)
                for m in range(n, 3):
                    ins = pool.tensor_copy(BIAS[parts[m], :], BIAS_F32[parts[m], :])
                chain.link(ins)
            pool.memset(XG, 0.0).then_inc(bias_ready, 1)
            pool.wait_ge(lists_ready, 1)
            n_blocks = pool.value_load(N_BLOCKS[0:1, 0:1], min_val=TOKENS * TOP_K // P, max_val=MAX_BLOCKS)

            def gather(col):
                chain.link(pool.tensor_copy(GATHER_AT, TOKEN[:, col]))
                pool.sem_inc(index_set, 1)
                pool.indirect_dma_start(out=XG, out_offset=None, in_=h2_dram,
                                        in_offset=bass.IndirectOffsetOnAxis(ap=GATHER_AT, axis=0),
                                        bounds_check=TOKENS - 1, oob_is_err=False).then_inc(gathered, 16)

            pool.wait_ge(s_h2, 32)
            pool.wait_ge(bias_ready, 1)
            gather(slice(0, 1))
            with chain.fori(n_blocks, 2) as i:
                pool.wait_ge(x_turned, i * 2 + 2)
                gather(bass.ds(i + 1, 1))
                pool.wait_ge(y_ready, i * 2 + 4)
                chain.link(pool.tensor_copy(SCATTER_AT, ASSIGN[:, bass.ds(i, 1)]))
                pool.sem_inc(index_set, 1)
                pool.indirect_dma_start(out=ys_dram, out_offset=bass.IndirectOffsetOnAxis(ap=SCATTER_AT, axis=0),
                                        in_=YB, in_offset=None,
                                        bounds_check=TOKENS * TOP_K - 1, oob_is_err=False).then_inc(scattered, 16)
                pool.wait_ge(scattered, i * 16 + 16)
                pool.sem_inc(y_stored, 1)

        block = ctx.enter_context(nc.Block())

        @block.sync
        def _(sp):
            sync_mixer(sp)
            sync_experts(sp)

        @block.tensor
        def _(pe):
            tensor_mixer(pe)
            tensor_experts(pe)

        @block.scalar
        def _(act):
            chain = Chain(act, act_order)
            scalar_mixer(act, chain)
            scalar_experts(act, chain)

        @block.vector
        def _(dve):
            chain = Chain(dve, dve_order)
            vector_mixer(dve, chain)
            vector_experts(dve, chain)

        @block.gpsimd
        def _(pool):
            chain = Chain(pool, pool_order)
            pool_mixer(pool, chain)
            pool_experts(pool, chain)


def kernel(**inputs):
    import concourse.bacc as bacc
    from concourse.bass_utils import run_bass_kernel_spmd

    a = {k: np.asarray(v) for k, v in inputs.items()}

    def by_channel(v):
        v = v.reshape(v.shape[:-1] + (v.shape[-1] // P, P))
        return np.moveaxis(np.moveaxis(v, -1, 0), -1, 1)

    arrays = {
        "x_all": np.concatenate([a["x_prompt"][0], a["x_sample"].reshape(NS, D_MODEL)], 0),
        "cst": constants()[0],
        "parc": np.concatenate([by_channel(v).reshape(P, -1) for v in (
            a["conv_w"][0], a["conv_b"][0], a["ssm_norm"][0], a["ret_norm"][0].reshape(-1), a["norm_mix"][0],
            a["norm_ffn"][0], a["state_conv"][0])], 1),
        "rowp": np.concatenate([a["dt_bias"][0], a["a_log"][0], a["d_skip"][0], a["b_router"][0]])[None],
        "norm_final": a["norm_final"][None],
        "w_in": a["w_in"][0],
        "w_out_ret": a["w_out_ret"][0],
        "w_out_ssm": a["w_out_ssm"][0],
        "w_out": a["w_out"][0],
        "w_router": a["w_router"][0],
        "ret_in": a["state_ret"][0],
        "ssm_in": a["state_ssm"][0].reshape(DEC_BATCH, INNER, DSTATE).transpose(0, 2, 1),
        "w_gate_up": a["w_gate_up"][0],
        "b_gate_up": a["b_gate_up"][0],
        "w_down": a["w_down"][0],
        "b_down": a["b_down"][0],
    }
    outs = {
        "y_out": (TOKENS, D_MODEL),
        "ret_p": (RET_HEADS, RET_DK, RET_DV),
        "ret_s": (DEC_BATCH, RET_HEADS, RET_DK, RET_DV),
        "ssm_p": (DSTATE, INNER),
        "ssm_s": (DEC_BATCH, DSTATE, INNER),
        "conv_p": (P, 24, TAPS - 1),
        "conv_s": (P, 24, DEC_BATCH, TAPS - 1),
    }
    nc = bacc.Bacc("TRN2", target_bir_lowering=False, num_devices=1)
    args, sent = [], {}
    for name, v in arrays.items():
        v = np.ascontiguousarray(v)
        sent["in_" + name] = v
        args.append(nc.dram_tensor("in_" + name, v.shape, mybir.dt.from_np(v.dtype), kind="ExternalInput").ap())
    for name, shape in outs.items():
        args.append(nc.dram_tensor("out_" + name, shape, F32, kind="ExternalOutput").ap())
    program(nc, *args)
    got = run_bass_kernel_spmd(nc, [sent], core_ids=[0]).results[0]
    g = {name: np.asarray(got["out_" + name]) for name in outs}

    def ssm_back(v):
        return np.ascontiguousarray(np.swapaxes(v, -1, -2)).reshape(v.shape[:-2] + (SSM_HEADS, HEADDIM, DSTATE))

    return (
        np.ascontiguousarray(g["y_out"][0:SEQ])[None],
        np.ascontiguousarray(g["y_out"][SEQ:]).reshape(DEC_BATCH, DEC_SEQ, D_MODEL),
        g["ret_p"][None, None],
        g["ret_s"][None],
        ssm_back(g["ssm_p"])[None, None],
        ssm_back(g["ssm_s"])[None],
        np.ascontiguousarray(g["conv_p"].transpose(2, 1, 0)).reshape(1, 1, TAPS - 1, CONV_DIM),
        np.ascontiguousarray(g["conv_s"].transpose(2, 3, 1, 0)).reshape(1, DEC_BATCH, TAPS - 1, CONV_DIM),
    )
```

```python
from contextlib import ExitStack, contextmanager
import math

import numpy as np

import concourse.bass as bass
from concourse import mybir

F32 = mybir.dt.float32
BF16 = mybir.dt.bfloat16
I32 = mybir.dt.int32
U32 = mybir.dt.uint32
ALU = mybir.AluOpType
ACT = mybir.ActivationFunctionType
AX = mybir.AxisListType

P = 128
D_MODEL = 1024
SEQ, DEC_BATCH, DEC_SEQ, PAST_LEN = 256, 8, 8, 2048
TOKENS = SEQ + DEC_BATCH * DEC_SEQ
TILES = 3
ROWS = (128, 128, 64)
TOK0 = (0, 128, 256)
SAMPLE = slice(SEQ, TOKENS)
NS = DEC_BATCH * DEC_SEQ
RET_HEADS, RET_DK, RET_DV = 4, 128, 256
SSM_HEADS, HEADDIM, GROUPS, DSTATE = 32, 64, 4, 128
HPG = SSM_HEADS // GROUPS
GW = HPG * HEADDIM
INNER = SSM_HEADS * HEADDIM
CONV_DIM = INNER + 2 * GROUPS * DSTATE
TAPS = 4
N_EXPERTS, TOP_K, D_FF = 32, 4, 1024
LIMIT, ALPHA = 7.0, 1.702
EPS = 1e-6
KT = D_MODEL // P
CH = 512
COL_Q, COL_V, COL_G, COL_Z = 0, 1024, 2048, 3072
COL_XBC = COL_Z + INNER
COL_DT = COL_XBC + CONV_DIM
COL_GATES = COL_DT + SSM_HEADS
LANES = 64
MAX_BLOCKS = (TOKENS * TOP_K - N_EXPERTS) // LANES + N_EXPERTS + 1
MIN_BLOCKS = TOKENS * TOP_K // LANES
BLOCK_COLS = MAX_BLOCKS + 2 + MAX_BLOCKS % 2
NOWHERE = float(1 << 20)
NEG = -1.0e30
PROMPT_RAW = TAPS - 1 + SEQ
SAMPLE_RAW = DEC_BATCH * (TAPS - 1 + DEC_SEQ)
RAW = PROMPT_RAW + 1 + SAMPLE_RAW


def constants():
    f = np.float32
    i, j = np.meshgrid(np.arange(P), np.arange(P))
    js, is_ = j[:NS, :NS], i[:NS, :NS]
    same = js // DEC_SEQ == is_ // DEC_SEQ
    gamma = 1.0 - 2.0 ** (-5.0 - np.arange(RET_HEADS))
    lg = np.log(gamma)
    scale = RET_DK ** -0.5

    def rows(a):
        out = np.zeros((P, a.shape[1]), f)
        out[:a.shape[0]] = a
        return out

    inv = 1.0 / (10000.0 ** np.linspace(0.0, 1.0, RET_DK // 2, dtype=f))
    pos = np.zeros((TILES, P))
    pos[0], pos[1] = np.arange(P), np.arange(P) + P
    pos[2, :NS] = PAST_LEN + np.arange(NS) % DEC_SEQ
    ang = (pos.astype(f)[:, :, None] * inv.astype(f)[None, None, :]).astype(f).astype(np.float64)
    loc = np.arange(NS) % DEC_SEQ
    parts = {
        "ident": np.eye(P),
        "upto": (j <= i),
        "before": (j < i),
        "ones": np.ones((P, P)),
        "upto_s": rows((js <= is_) & same),
        "ones_s": rows(same),
        "mask": np.where(i >= j, 0.0, NEG),
        "mask_s": rows(np.where((is_ >= js) & same, 0.0, NEG)),
        "decay": np.concatenate([np.where(i >= j, np.exp(lg[h] * np.maximum(i - j, 0)), 0.0) * scale
                                 for h in range(RET_HEADS)], 1),
        "decay_s": rows(np.concatenate([np.where((is_ >= js) & same, np.exp(lg[h] * np.maximum(is_ - js, 0)), 0.0)
                                        * scale for h in range(RET_HEADS)], 1)),
        "q_decay": np.tile(np.concatenate([np.exp(lg[h] * (np.concatenate([np.arange(P), loc]) + 1.0))
                                           for h in range(RET_HEADS)])[None], (P, 1)),
        "seq_cols": np.tile((np.arange(DEC_BATCH)[:, None] == np.arange(NS)[None] // DEC_SEQ).reshape(1, -1), (P, 1)),
        "cos": np.concatenate(list(np.cos(ang)), 1),
        "sin": np.concatenate(list(np.sin(ang)), 1),
        "k_decay": np.exp(lg[None] * (P - 1.0 - np.arange(P)[:, None])) * scale,
        "k_decay_s": rows(np.exp(lg[None] * (DEC_SEQ - 1.0 - loc[:, None])) * scale),
        "seq_rows": rows(np.arange(NS)[:, None] // DEC_SEQ == np.arange(DEC_BATCH)[None]),
        "experts": np.tile(np.arange(N_EXPERTS)[None], (P, 1)),
        "blocks": np.tile(np.arange(BLOCK_COLS)[None], (P, 1)),
        "assign": np.concatenate([(TOK0[t] + np.arange(P))[:, None] * TOP_K + np.arange(TOP_K)[None] + 1
                                  for t in range(TILES)], 1),
        "lanes": np.tile(np.arange(P)[None] % LANES, (P, 1)),
        "half": (np.arange(P) // LANES)[:, None],
        "mod32": (np.arange(P) % N_EXPERTS)[:, None],
    }
    at, n = {}, 0
    for name, a in parts.items():
        at[name] = n
        n += a.shape[1]
    return np.ascontiguousarray(np.concatenate([np.asarray(a, f) for a in parts.values()], 1)), at, n


RET_GAMMA = [1.0 - 2.0 ** (-5.0 - h) for h in range(RET_HEADS)]


class Chain:

    def __init__(self, eng, sem):
        self.eng, self.sem, self.n, self.at = eng, sem, 0, 0

    def link(self, ins):
        ins.then_inc(self.sem, 1)
        self.n += 1
        self.eng.wait_ge(self.sem, self.at + self.n)

    @contextmanager
    def fori(self, count, links):
        with self.eng.Fori(0, count) as i:
            first = self.n
            self.at = i * links
            yield i
            assert self.n - first == links, (self.n - first, links)
        if isinstance(count, int):
            self.at = 0
            self.n += links * (count - 1)
        else:
            self.at = (count - 1) * links


def program(nc, x_all, cst, parc, rowp, norm_final, w_in, w_out_ret, w_out_ssm, w_out, w_router,
            ret_in, ssm_in, w_gate_up, b_gate_up, w_down, b_down,
            y_out, ret_p, ret_s, ssm_p, ssm_s, conv_p, conv_s):
    _, C, CW = constants()
    with ExitStack() as ctx:
        def sb(name, shape, dt=F32):
            return ctx.enter_context(nc.sbuf_tensor(name, shape, dt))

        def sem(name):
            return ctx.enter_context(nc.semaphore(name))

        CST = sb("CST", [P, CW])
        X = sb("X", [P, TILES, D_MODEL])
        PARC = sb("PARC", [P, 24 * TAPS + 24 + 16 + 8 + 8 + 8 + 24 * 24])
        ROWP = sb("ROWP", [P, 4, 32])
        WDT = sb("WDT", [P, KT, SSM_HEADS])
        WR = sb("WR", [P, KT, N_EXPERTS])
        ARENA = sb("ARENA", [P, 38656])
        TEMPS = sb("TEMPS", [P, 4608])
        SMALL = sb("SMALL", [P, 1472])

        def const(name, width, r=P, start=0):
            return CST[0:r, C[name] + start:C[name] + start + width]

        o = 0
        conv_w = PARC[:, o:o + 96].rearrange("p (m i) -> p m i", i=TAPS)
        o += 96
        conv_b = PARC[:, o:o + 24]
        o += 24
        ssm_norm = PARC[:, o:o + 16]
        o += 16
        ret_norm = PARC[:, o:o + 8]
        o += 8
        norm_mix = PARC[:, o:o + 8]
        o += 8
        norm_ffn = PARC[:, o:o + 8]
        o += 8
        conv_state = PARC[:, o:o + 576].rearrange("p (m b i) -> p m b i", b=DEC_BATCH, i=TAPS - 1)
        dt_bias, a_log, d_skip, b_router = (ROWP[:, n, :] for n in range(4))

        def region(a, n):
            return ARENA[:, a:a + n]

        W = [region(4096 * s, 4096).rearrange("p (k n) -> p k n", k=KT) for s in range(2)]
        W16 = [region(4096 * s, 4096).rearrange("p (k n) -> p k n", k=2 * KT) for s in range(2)]
        HT = region(8192, 2560).rearrange("p (k n) -> p k n", k=KT)
        XBC = region(10752, 24 * TOKENS).rearrange("p (m n) -> p m n", m=24)
        QKV = region(18432, 6144).rearrange("p (t n) -> p t n", t=TILES)
        XS = region(24576, 6144).rearrange("p (t n) -> p t n", t=TILES)
        BTOK = region(30720, 1536).rearrange("p (t n) -> p t n", t=TILES)
        QKT = region(32256, 2560).rearrange("p (h n) -> p h n", h=2 * RET_HEADS)
        QTD = region(34816, 768).rearrange("p (h n) -> p h n", h=RET_HEADS)
        O = region(35584, 3072).rearrange("p (t n) -> p t n", t=TILES)
        H = region(24576, 3072).rearrange("p (t n) -> p t n", t=TILES)
        RAWB = region(35584, 2 * 4 * RAW).rearrange("p (s m n) -> p s m n", s=2, m=4)
        SSM_IN = [region(3072 * s, 2048) for s in range(2)]
        RET_IN = [region(3072 * s + 2048, 1024) for s in range(2)]
        SSM_PR = region(35584, 2048)
        XDT = region(10752, 2048)
        XEND = region(12800, 2048)
        RET_PR = region(14848, 1024)
        Z = region(10752, 6144).rearrange("p (t n) -> p t n", t=TILES)
        YT = region(10752, 5120).rearrange("p (k n) -> p k n", k=16)
        OT = region(15872, 2560).rearrange("p (k n) -> p k n", k=8)
        SG = region(18432, 5120).rearrange("p (m n) -> p m n", m=16)
        MERGED = region(32256, 2560).rearrange("p (k n) -> p k n", k=KT)

        ROT = TEMPS[:, 0:2048].rearrange("p (a n) -> p a n", a=4)
        SEG = TEMPS[:, 0:2048].rearrange("p (s h n) -> p s h n", s=2, h=HPG)
        CTM = [TEMPS[:, 1536 * s:1536 * s + 256].rearrange("p (g n) -> p g n", g=4) for s in range(2)]
        QTM = [TEMPS[:, 1536 * s + 256:1536 * s + 512].rearrange("p (g n) -> p g n", g=4) for s in range(2)]
        BM = [TEMPS[0:NS, 1536 * s + 512:1536 * s + 1024] for s in range(2)]
        KM = [TEMPS[0:NS, 1536 * s + 1024:1536 * s + 1536] for s in range(2)]
        Z_STAGE = [TEMPS[:, 2048 + 512 * s:2560 + 512 * s] for s in range(2)]
        TMP = TEMPS[:, 3072:3584]
        KDEC = TEMPS[:, 3584:4096]
        SM = TEMPS[:, 4096:4608].rearrange("p (h n) -> p h n", h=RET_HEADS)
        SIL = [TEMPS[:, 3584 + 512 * s:4096 + 512 * s] for s in range(2)]
        SQ = TEMPS[:, 0:1024]

        o = 0

        def small(n):
            nonlocal o
            o += n
            assert o <= 1472
            return SMALL[:, o - n:o]

        RMS = small(32)
        DTW = small(96 * 6).rearrange("p (a n) -> p a n", a=6)
        DT, DTA, CUM, ECUM, TOEND, LNW = (DTW[:, n, :].rearrange("p (t h) -> p t h", t=TILES) for n in range(6))
        NA = small(32)
        DEC_P = small(32)
        DEC_S = small(256).rearrange("p (b h) -> p b h", b=DEC_BATCH)
        CONV_TAIL = small(24 * 3).rearrange("p (m i) -> p m i", i=3)
        CONV_TAIL_S = PARC[:, 160:160 + 576].rearrange("p (m b i) -> p m b i", b=DEC_BATCH, i=TAPS - 1)

        PS = [ctx.enter_context(nc.psum_tensor(f"PS{n}", [P, 512], F32)) for n in range(8)]
        s_x, s_cst, s_par, s_wdt = sem("x_in"), sem("constants_in"), sem("parameters_in"), sem("w_dt_in")
        s_w = [sem(f"weights_in_{s}") for s in range(2)]
        s_st_in = [sem(f"states_in_{s}") for s in range(2)]
        s_st_out = [sem(f"states_out_{s}") for s in range(2)]
        s_small_out, s_ssm_p = sem("small_out"), sem("ssm_p_out")
        s_z_out, s_z_in = [sem(f"z_out_{s}") for s in range(2)], sem("z_in")
        dve_order, act_order, pool_order = sem("dve_order"), sem("act_order"), sem("pool_order")
        rms_init = sem("rms_init")
        squares, variance, deviation = sem("squares"), sem("variance"), sem("deviation")
        h_ready, h_turned, ht_ready = sem("h_ready"), sem("h_turned"), sem("ht_ready")
        xbc_mm, raw_ready, pads_ready, tails_done, conv_done = (
            sem("xbc_mm"), sem("raw_ready"), sem("pads_ready"), sem("tails_done"), sem("conv_done"))
        silu_xbc = sem("silu_xbc")
        dt_mm, dt_arg, dt_exp, dt_w, dt_ln, na_ready, dta_ready = (
            sem("dt_mm"), sem("dt_arg"), sem("dt_exp"), sem("dt_w"), sem("dt_ln"), sem("na_ready"), sem("dta_ready"))
        qkv_mm, qkv_evac, rotated = sem("qkv_mm"), sem("qkv_evac"), sem("rotated")
        turn_mm, turn_evac = sem("turn_mm"), sem("turn_evac")
        cum_mm, cum_read, cum_exp, toend_ready = sem("cum_mm"), sem("cum_read"), sem("cum_exp"), sem("toend_ready")
        seg_mm, seg_sub, seg_exp, wts_ready = sem("seg_mm"), sem("seg_sub"), sem("seg_exp"), sem("wts_ready")
        xdt_ready, back_mm, y_evac = sem("xdt_ready"), sem("back_mm"), sem("y_evac")
        qtd_ready, kdec_ready = sem("qtd_ready"), sem("kdec_ready")
        score_mm, score_ready, ret_mm, ret_evac = sem("score_mm"), sem("score_ready"), sem("ret_mm"), sem("ret_evac")
        zero_ready = sem("zero_ready")
        masks_ready, cross_mm, upd_mm, upd_evac, closed = (
            sem("masks_ready"), sem("cross_mm"), sem("upd_mm"), sem("upd_evac"), sem("closed"))
        sample_y = sem("sample_y")
        g_mm, sil_ready, sil_used = sem("g_mm"), sem("sil_ready"), sem("sil_used")
        z_mm, z_staged, z_silu, z_used = sem("z_mm"), sem("z_staged"), sem("z_silu"), sem("z_used")
        gate_mm, gate_evac = sem("gate_mm"), sem("gate_evac")
        y_scaled, turn2_mm, turn2_evac = sem("y_scaled"), sem("turn2_mm"), sem("turn2_evac")
        oa_mm, oa_evac, ob_mm, ob_evac, out_mm, x1_ready = (
            sem("oa_mm"), sem("oa_evac"), sem("ob_mm"), sem("ob_evac"), sem("out_mm"), sem("x1_ready"))

        ZERO = small(256)[0:1, :].bitcast(BF16)
        UNITS = [(t, g) for t in range(TILES) for g in range(GROUPS)]

        def heads(ap, n, width):
            return ap.unsqueeze(2).to_broadcast([ap.shape[0], n, width])

        z_dram = nc.dram_tensor("z_rows", (TOKENS, INNER), F32).ap()
        BESIDE_QKV = ([("x", i) for i in range(9)] + [("sums", 0)] + [("x", i) for i in range(9, 12)]
                      + [("b", i) for i in range(3)] + [(None, 0)] * 2 + [("qk", i) for i in range(6)])
        TURNS = [step for step in BESIDE_QKV if step[0] in ("x", "b", "qk")]

        def turn_bank(kind):
            return PS[7] if kind == "x" else PS[3]

        def turns_to(kind, i):
            return TURNS.index((kind, i)) + 1

        def quads(bank):
            return bank[:, :].rearrange("p (q n) -> p q n", q=4)

        def w_cols(w, start, width=CH):
            return w[:, start:start + width].rearrange("(k p) n -> p k n", p=P)

        def w_ds(w, at, width=CH):
            return w[:, bass.ds(at, width)].rearrange("(k p) n -> p k n", p=P)

        def sync_mixer(sp):
            sp.dma_start(X[:, 0:2, :], x_all[0:SEQ, :].rearrange("(t p) d -> p t d", p=P)).then_inc(s_x, 16)
            sp.dma_start(X[0:NS, 2, :], x_all[SAMPLE, :]).then_inc(s_x, 16)
            sp.dma_start(CST[:, :], cst).then_inc(s_cst, 16)
            sp.dma_start(PARC[:, :], parc).then_inc(s_par, 16)
            sp.dma_start(ROWP[:, :, :].rearrange("p a b -> p (a b)"), rowp.to_broadcast([P, 128])).then_inc(s_par, 16)
            sp.dma_start(WDT[:, :, :], w_cols(w_in, COL_DT, SSM_HEADS)).then_inc(s_wdt, 16)
            sp.dma_start(WR[:, :, :], w_cols(w_router, 0, N_EXPERTS)).then_inc(s_wdt, 16)

            def stream(col, rounds, used, per_chunk, before):
                for s in range(2):
                    if before is not None:
                        sp.wait_ge(*before[s])
                    sp.dma_start(W[s], w_cols(w_in, col + CH * s)).then_inc(s_w[s], 16)
                if rounds > 1:
                    with sp.Fori(0, rounds - 1) as j:
                        for s in range(2):
                            sp.wait_ge(used, j * (2 * per_chunk) + per_chunk * (s + 1))
                            sp.dma_start(W[s], w_ds(w_in, j * (2 * CH) + (col + CH * (s + 2)))).then_inc(s_w[s], 16)

            stream(COL_XBC, 3, xbc_mm, 4, None)
            stream(COL_Q, 2, qkv_mm, 3, [(xbc_mm, 20), (xbc_mm, 24)])

            def state_in(p, ssm, ret):
                sp.dma_start(SSM_IN[p], ssm).then_inc(s_st_in[p], 16)
                sp.dma_start(RET_IN[p].rearrange("p (h n) -> p h n", h=RET_HEADS), ret).then_inc(s_st_in[p], 16)

            def state_out(p, ssm, ret):
                sp.dma_start(ssm, SSM_IN[p]).then_inc(s_st_out[p], 16)
                sp.dma_start(ret, RET_IN[p].rearrange("p (h n) -> p h n", h=RET_HEADS)).then_inc(s_st_out[p], 16)

            sp.wait_ge(tails_done, 8 + 24)
            sp.dma_start(conv_p, CONV_TAIL).then_inc(s_small_out, 16)
            sp.dma_start(conv_s, CONV_TAIL_S).then_inc(s_small_out, 16)
            for s in range(2):
                sp.wait_ge(qkv_mm, 9 + 3 * s)
                sp.dma_start(W[s], w_cols(w_in, COL_Z + CH * s)).then_inc(s_w[s], 16)
            for i in range(12):
                c, t = i // 3, i % 3
                r = ROWS[t]
                sp.wait_ge(z_staged, i + 1)
                sp.dma_start(z_dram[TOK0[t]:TOK0[t] + r, CH * c:CH * (c + 1)],
                             Z_STAGE[i % 2][0:r, :]).then_inc(s_z_out[i % 2], 16)
                if t == 2 and c < 2:
                    sp.dma_start(W[c], w_cols(w_in, COL_Z + CH * (c + 2))).then_inc(s_w[c], 16)
                if t == 2 and c >= 2:
                    state_in(c - 2, ssm_in[c - 2], ret_in[c - 2].rearrange("h d v -> d h v"))
                if i == 9:
                    sp.wait_ge(y_evac, 8)
                    sp.dma_start(ssm_p, SSM_PR).then_inc(s_ssm_p, 16)
            sp.wait_ge(ret_evac, 4)
            sp.dma_start(ret_p.rearrange("h d v -> d h v"),
                         RET_PR.rearrange("p (h n) -> p h n", h=RET_HEADS)).then_inc(s_small_out, 16)
            ssm_i = ssm_in.rearrange("b n q -> n b q")
            ret_i = ret_in.rearrange("b h d v -> d b h v")
            ssm_o = ssm_s.rearrange("b n q -> n b q")
            ret_o = ret_s.rearrange("b h d v -> d b h v")
            with sp.Fori(0, DEC_BATCH // 2 - 1) as j:
                for p in range(2):
                    sp.wait_ge(upd_evac, j * 12 + (6 * p + 8))
                    state_out(p, ssm_o[:, bass.ds(j * 2 + p, 1), :].squeeze(1),
                              ret_o[:, bass.ds(j * 2 + p, 1), :, :].squeeze(1))
                    sp.wait_ge(s_st_out[p], j * 32 + 32)
                    state_in(p, ssm_i[:, bass.ds(j * 2 + (p + 2), 1), :].squeeze(1),
                             ret_i[:, bass.ds(j * 2 + (p + 2), 1), :, :].squeeze(1))
            for p in range(2):
                b = DEC_BATCH - 2 + p
                sp.wait_ge(upd_evac, 6 * (b + 1) + 2)
                state_out(p, ssm_s[b], ret_s[b].rearrange("h d v -> d h v"))
            for p in range(2):
                sp.wait_ge(s_st_out[p], 32 * (DEC_BATCH // 2))
            sp.wait_ge(s_small_out, 48)
            stream(COL_G, 1, None, 3, None)
            for p in range(2):
                sp.wait_ge(s_z_out[p], 16 * 6)
            for t in range(TILES):
                r = ROWS[t]
                sp.dma_start(Z[0:r, t, :], z_dram[TOK0[t]:TOK0[t] + r, :]).then_inc(s_z_in, 16)
            stream(COL_GATES, 2, gate_mm, 4, [(g_mm, 3), (g_mm, 6)])
            for s in range(2):
                sp.wait_ge(gate_mm, 12 + 4 * s)
                sp.dma_start(W[s], w_cols(w_out_ret, CH * s)).then_inc(s_w[s], 16)
            for s in range(2):
                sp.wait_ge(oa_mm, 4 + 4 * s)
                sp.dma_start(W16[s], w_cols(w_out_ssm, 256 * s, 256)).then_inc(s_w[s], 16)
            for s in range(2):
                sp.wait_ge(ob_mm, 2 + 2 * s)
                sp.dma_start(W16[s], w_cols(w_out_ssm, 256 * (s + 2), 256)).then_inc(s_w[s], 16)
            for s in range(2):
                sp.wait_ge(ob_mm, 6 + 2 * s)
                sp.dma_start(W[s], w_cols(w_out, CH * s)).then_inc(s_w[s], 16)

        def tensor_mixer(pe):
            pe.wait_ge(s_cst, 16)
            ident = const("ident", P)
            for n in range(6):
                t, k0 = n // 2, 4 * (n % 2)
                r = ROWS[t]
                pe.wait_ge(h_ready, t + 1)
                for k in range(4):
                    mm = pe.transpose(quads(PS[n])[:, k, 0:r], H[0:r, t, P * (k0 + k):P * (k0 + k + 1)],
                                      const("ident", r, r))
                mm.then_inc(h_turned, 1)
            pe.wait_ge(ht_ready, 6)

            with pe.Fori(0, 3) as j:
                for s in range(2):
                    pe.wait_ge(s_w[s], j * 16 + 16)
                    for m in range(4):
                        pe.wait_ge(raw_ready, j * 8 + (4 * s + m + 1))
                        for k in range(KT):
                            mm = pe.matmul(PS[4 * s + m][:, 0:TOKENS], W[s][:, k, P * m:P * (m + 1)], HT[:, k, :],
                                           start=(k == 0), stop=(k == KT - 1))
                        mm.then_inc(xbc_mm, 1)

            def by_token(bank, t, w, src, ks=range(KT)):
                r = ROWS[t]
                for k in ks:
                    tokens = src[:, k, TOK0[t]:TOK0[t] + r]
                    if r == P:
                        mm = pe.matmul(bank[:, :], tokens, w[:, k, :], start=(k == 0), stop=(k == KT - 1))
                    else:
                        for h in range(2):
                            mm = pe.matmul(bank[NS * h:NS * (h + 1), 0:CH // 2], tokens,
                                           w[:, k, CH // 2 * h:CH // 2 * (h + 1)],
                                           start=(k == 0), stop=(k == KT - 1), tile_position=(0, NS * h))
                return mm

            pe.wait_ge(raw_ready, 8 + 24)
            pe.wait_ge(s_wdt, 32)
            for t in range(TILES):
                r = ROWS[t]
                for k in range(KT):
                    mm = pe.matmul(PS[3][0:r, 32 * t:32 * t + 32], HT[:, k, TOK0[t]:TOK0[t] + r], WDT[:, k, :],
                                   start=(k == 0), stop=(k == KT - 1))
            mm.then_inc(dt_mm, 1)

            def running_sums():
                pe.wait_ge(dta_ready, 1)
                bank = PS[3]
                for t in range(TILES):
                    r = ROWS[t]
                    upto, ones = (("upto", "ones"), ("upto_s", "ones_s"))[t == 2]
                    pe.matmul(bank[0:r, 32 * t:32 * t + 32], const(upto, r, r), DTA[0:r, t, :], start=True, stop=True)
                    pe.matmul(bank[0:r, 96 + 32 * t:128 + 32 * t], const(ones, r, r), DTA[0:r, t, :],
                              start=True, stop=True)
                for b in range(DEC_BATCH):
                    mm = pe.matmul(bank[:, 192 + 32 * b:224 + 32 * b],
                                   const("seq_rows", 1, NS, b).to_broadcast([NS, P]), DTA[0:NS, 2, :],
                                   start=True, stop=True)
                mm.then_inc(cum_mm, 1)

            turned = {}
            for place, (kind, i) in enumerate(BESIDE_QKV):
                tile, half = place // 2, place % 2
                c, t = tile // 3, tile % 3
                if half == 0:
                    if t == 0:
                        pe.wait_ge(s_w[c % 2], 16 * (4 + c // 2))
                    if tile >= 6:
                        pe.wait_ge(qkv_evac, tile - 5)
                mm = by_token(PS[4 * (c % 2) + t], t, W[c % 2], HT, range(4 * half, 4 * half + 4))
                if half == 1:
                    mm.then_inc(qkv_mm, 1)
                if kind is None:
                    continue
                if kind == "sums":
                    running_sums()
                    continue
                bank = turn_bank(kind)
                if kind in ("b", "qk") and not turned.get("PS3"):
                    pe.wait_ge(cum_read, 1)
                last = turned.get("PS7" if kind == "x" else "PS3")
                if last:
                    pe.wait_ge(turn_evac, last)
                turned["PS7" if kind == "x" else "PS3"] = turns_to(kind, i)
                if kind == "qk":
                    t, half = i // 2, i % 2
                    r = ROWS[t]
                    pe.wait_ge(rotated, t + 1)
                    for h in range(RET_HEADS):
                        mm = pe.transpose(quads(bank)[:, h, 0:r],
                                          QKV[0:r, t, 512 * half + P * h:512 * half + P * (h + 1)],
                                          const("ident", r, r))
                else:
                    t, m0 = (i // 4, 4 * (i % 4)) if kind == "x" else (i, 16)
                    r = ROWS[t]
                    pe.wait_ge(silu_xbc, 2 if kind == "x" else 3)
                    for m in range(4):
                        mm = pe.transpose(bank[0:r, P * m:P * (m + 1)], XBC[:, m0 + m, TOK0[t]:TOK0[t] + r], ident)
                mm.then_inc(turn_mm, 1)
            pe.wait_ge(qkv_evac, 12)

            def front(u):
                t, g = UNITS[u]
                r = ROWS[t]
                tok = slice(TOK0[t], TOK0[t] + r)
                upto = const("upto_s" if t == 2 else "upto", r, r)
                if u >= 1:
                    pe.wait_ge(seg_sub, 2 * u)
                if u >= 2:
                    pe.wait_ge(wts_ready, u - 1)
                pe.matmul(PS[4][0:r, P * (u % 2):P * (u % 2) + r], XBC[:, 16 + g, tok], XBC[:, 20 + g, tok],
                          start=True, stop=True)
                for h in range(HPG):
                    mm = pe.matmul(quads(PS[h // 4])[0:r, h % 4, 0:r],
                                   DTA[0:r, t, HPG * g + h:HPG * g + h + 1].to_broadcast([r, r]), upto,
                                   start=True, stop=True)
                    if h % 4 == 3:
                        mm.then_inc(seg_mm, 1)

            def back(u):
                t, g = UNITS[u]
                r = ROWS[t]
                cols = slice(GW * g, GW * (g + 1))
                pe.wait_ge(wts_ready, u + 1)
                pe.wait_ge(xdt_ready, u + 1)
                if u >= 1:
                    pe.wait_ge(y_evac, u)
                for h in range(HPG):
                    at = GW * g + HEADDIM * h
                    mm = pe.matmul(PS[5][0:r, HEADDIM * h:HEADDIM * (h + 1)], SEG[0:r, u % 2, h, 0:r],
                                   XDT[0:r, at:at + HEADDIM], start=True, stop=True)
                if t == 1:
                    pe.matmul(PS[6][0:r, :], XBC[:, 20 + g, P:2 * P], SSM_PR[:, cols], start=True, stop=True)
                if t < 2:
                    mm = pe.matmul(PS[7][:, :], BTOK[0:r, t, P * g:P * (g + 1)], XEND[0:r, cols],
                                   start=True, stop=True)
                mm.then_inc(back_mm, 1)

            pe.wait_ge(cum_read, 1)
            pe.wait_ge(turn_evac, 21)
            front(0)
            for u in range(len(UNITS)):
                if u + 1 < len(UNITS):
                    front(u + 1)
                c, t = u // 3, u % 3
                if t == 0:
                    pe.wait_ge(s_w[c % 2], 16 * (6 + c // 2))
                if u >= 2:
                    pe.wait_ge(z_staged, u - 1)
                by_token(PS[2 + u % 2], t, W[c % 2], HT).then_inc(z_mm, 1)
                back(u)

            def scores(t, bank):
                r = ROWS[t]
                tok = slice(TOK0[t], TOK0[t] + r)
                for h in range(RET_HEADS):
                    mm = pe.matmul(quads(bank)[0:r, h, 0:r], QKT[:, RET_HEADS + h, tok], QKT[:, h, tok],
                                   start=True, stop=True)
                mm.then_inc(score_mm, 1)

            def retain(t, banks, carried, open_end):
                r = ROWS[t]
                pe.wait_ge(score_ready, t + 1)
                for h in range(RET_HEADS):
                    out = banks[h // 2][0:r, RET_DV * (h % 2):RET_DV * (h % 2 + 1)]
                    v = QKV[0:r, t, 1024 + RET_DV * h:1024 + RET_DV * (h + 1)]
                    if open_end:
                        mm = pe.matmul(out, SM[0:r, h, 0:r], v, start=(h % 2 == 0), stop=False,
                                       skip_group_check=True)
                        continue
                    mm = pe.matmul(out, SM[0:r, h, 0:r], v, start=True, stop=not carried)
                    if carried:
                        mm = pe.matmul(out, QTD[:, h, 0:P], RET_PR[:, RET_DV * h:RET_DV * (h + 1)],
                                       start=False, stop=True)
                mm.then_inc(ret_mm, 1)

            def keep(t):
                pe.wait_ge(kdec_ready, t + 1)
                for h in range(RET_HEADS):
                    mm = pe.matmul(PS[3 + h // 2][:, RET_DV * (h % 2):RET_DV * (h % 2 + 1)],
                                   KDEC[:, P * h:P * (h + 1)],
                                   QKV[:, t, 1024 + RET_DV * h:1024 + RET_DV * (h + 1)], start=True, stop=True)
                mm.then_inc(ret_mm, 1)

            pe.wait_ge(y_evac, 12)
            pe.wait_ge(z_staged, 12)
            pe.wait_ge(qtd_ready, 1)
            scores(0, PS[0])
            scores(1, PS[5])
            retain(0, (PS[1], PS[2]), False, False)
            keep(0)
            pe.wait_ge(ret_evac, 2)
            retain(1, (PS[6], PS[7]), True, False)
            keep(1)
            scores(2, PS[5])
            pe.wait_ge(ret_evac, 3)
            retain(2, (PS[0], PS[1]), False, True)

            pe.wait_ge(ret_evac, 4)
            pe.wait_ge(zero_ready, 1)
            for g in range(GROUPS):
                pe.matmul(PS[2 + g][0:NS, :], ZERO[:, 0:NS], ZERO[:, :], start=True, stop=False,
                          skip_group_check=True)
            with pe.Fori(0, DEC_BATCH // 2) as j:
                for p in range(2):
                    pe.wait_ge(masks_ready, j * 2 + (p + 1))
                    pe.wait_ge(s_st_in[p], j * 32 + 32)
                    for g in range(GROUPS):
                        pe.matmul(PS[2 + g][0:NS, :], CTM[p][:, g, :], SSM_IN[p][:, GW * g:GW * (g + 1)],
                                  start=False, stop=False, skip_group_check=True)
                    for h in range(RET_HEADS):
                        mm = pe.matmul(PS[h // 2][0:NS, RET_DV * (h % 2):RET_DV * (h % 2 + 1)], QTM[p][:, h, :],
                                       RET_IN[p][:, RET_DV * h:RET_DV * (h + 1)],
                                       start=False, stop=False, skip_group_check=True)
                    mm.then_inc(cross_mm, 1)
                    for u in range(6):
                        bank = PS[6 + u % 2]
                        pe.wait_ge(upd_evac, j * 12 + (6 * p + u + 1))
                        if u < 4:
                            mm = pe.matmul(bank[:, :], BM[p][:, P * u:P * (u + 1)],
                                           XEND[0:NS, GW * u:GW * (u + 1)], start=True, stop=True)
                        else:
                            for e in range(2):
                                h = 2 * (u - 4) + e
                                mm = pe.matmul(bank[:, RET_DV * e:RET_DV * (e + 1)], KM[p][:, P * h:P * (h + 1)],
                                               QKV[0:NS, 2, 1024 + RET_DV * h:1024 + RET_DV * (h + 1)],
                                               start=True, stop=True)
                        mm.then_inc(upd_mm, 1)
            for n in range(6):
                mm = pe.matmul(PS[n][0:NS, :], ZERO[:, 0:NS], ZERO[:, :], start=False, stop=True,
                               skip_group_check=True)
            mm.then_inc(closed, 1)

            pe.wait_ge(sample_y, 1)
            for s in range(2):
                pe.wait_ge(s_w[s], 16 * 8)
                for t in range(TILES):
                    by_token(PS[4 * s + t], t, W[s], HT).then_inc(g_mm, 1)
            with pe.Fori(0, 2) as j:
                for s in range(2):
                    pe.wait_ge(s_w[s], j * 16 + 16 * 9)
                    pe.wait_ge(sil_ready, 3 * s + 3)
                    for m in range(4):
                        pe.wait_ge(gate_evac, j * 8 + (4 * s + m + 1))
                        for k in range(KT):
                            mm = pe.matmul(PS[4 * s + m][:, 0:TOKENS], W[s][:, k, P * m:P * (m + 1)], HT[:, k, :],
                                           start=(k == 0), stop=(k == KT - 1))
                        mm.then_inc(gate_mm, 1)
            pe.wait_ge(gate_evac, 8 + 16)
            for n in range(18):
                if n >= 4:
                    pe.wait_ge(turn2_evac, n - 3)
                t, q = (n // 4, n % 4) if n < 12 else ((n - 12) // 2, n % 2)
                r = ROWS[t]
                pe.wait_ge(y_scaled, t + 1)
                src = XS if n < 12 else O
                for m in range(4):
                    mm = pe.transpose(quads(PS[n % 4])[:, m, 0:r], src[0:r, t, P * (4 * q + m):P * (4 * q + m + 1)],
                                      const("ident", r, r))
                mm.then_inc(turn2_mm, 1)
            pe.wait_ge(turn2_evac, 18)
            for s in range(2):
                pe.wait_ge(s_w[s], 16 * 11)
                for m in range(4):
                    for k in range(KT):
                        mm = pe.matmul(PS[4 * s + m][:, 0:TOKENS], W[s][:, k, P * m:P * (m + 1)], OT[:, k, :],
                                       start=(k == 0), stop=(k == KT - 1))
                    mm.then_inc(oa_mm, 1)
            pe.wait_ge(oa_evac, 8)
            with pe.Fori(0, 2) as j:
                for s in range(2):
                    pe.wait_ge(s_w[s], j * 16 + 16 * 12)
                    for m in range(2):
                        pe.wait_ge(ob_evac, j * 4 + (2 * s + m + 1))
                        for k in range(16):
                            mm = pe.matmul(PS[4 * s + m][:, 0:TOKENS], W16[s][:, k, P * m:P * (m + 1)], YT[:, k, :],
                                           start=(k == 0), stop=(k == 15))
                        mm.then_inc(ob_mm, 1)
            pe.wait_ge(ob_evac, 4 + 8)
            for s in range(2):
                pe.wait_ge(s_w[s], 16 * 14)
                for t in range(TILES):
                    by_token(PS[4 * s + t], t, W[s], MERGED).then_inc(out_mm, 1)

        def token_parts(bank, t):
            if ROWS[t] == P:
                return [(slice(0, CH), bank[:, :])]
            return [(slice(CH // 2 * h, CH // 2 * (h + 1)), bank[NS * h:NS * (h + 1), 0:CH // 2]) for h in range(2)]

        def scalar_mixer(act, chain):
            summed = 0

            def square_sum(src, r, col, sink):
                nonlocal summed
                if summed:
                    act.wait_ge(squares, summed)
                summed += 1
                act.activation(sink, src, ACT.Square, accum_out=RMS[0:r, col:col + 1]).then_inc(squares, 1)

            act.sem_inc(raw_ready, 8)
            act.sem_inc(gate_evac, 8)
            act.wait_ge(rms_init, 1)
            for t in range(TILES):
                act.wait_ge(s_x, 32)
                r = ROWS[t]
                square_sum(X[0:r, t, :], r, t, SQ[0:r, :])
            act.wait_ge(variance, 1)
            act.activation(RMS[:, 0:3], RMS[:, 0:3], ACT.Sqrt).then_inc(deviation, 1)
            with act.Fori(0, 3) as j:
                for s in range(2):
                    for m in range(4):
                        raw = RAWB[:, s, m, :]
                        act.wait_ge(xbc_mm, j * 8 + (4 * s + m + 1))
                        act.wait_ge(conv_done, j * 8 + (4 * s + m + 1))
                        act.wait_ge(tails_done, j * 8 + (4 * s + m + 1))
                        act.activation(raw[:, TAPS - 1:PROMPT_RAW], PS[4 * s + m][:, 0:SEQ], ACT.Copy)
                        act.activation(
                            raw[:, PROMPT_RAW + 1:RAW].rearrange("p (b i) -> p b i", b=DEC_BATCH)[:, :, TAPS - 1:],
                            PS[4 * s + m][:, SAMPLE].rearrange("p (b i) -> p b i", b=DEC_BATCH),
                            ACT.Copy).then_inc(raw_ready, 1)
                act.wait_ge(conv_done, j * 8 + 16)
                v = XBC[:, bass.ds(j * 8, 8), :]
                act.activation(v, v, ACT.Silu).then_inc(silu_xbc, 1)
            act.wait_ge(s_par, 32)
            act.activation(NA, a_log, ACT.Exp).then_inc(na_ready, 1)
            for place, (kind, i) in enumerate(BESIDE_QKV):
                if kind in ("x", "b", "qk"):
                    act.wait_ge(turn_mm, turns_to(kind, i))
                    bank = turn_bank(kind)
                    if kind == "x":
                        t, q = i // 4, i % 4
                        dst, src = XS[0:ROWS[t], t, CH * q:CH * (q + 1)], bank[0:ROWS[t], :]
                    elif kind == "b":
                        dst, src = BTOK[0:ROWS[i], i, :], bank[0:ROWS[i], :]
                    else:
                        t, half = i // 2, i % 2
                        dst = QKT[:, 4 * half:4 * half + 4, TOK0[t]:TOK0[t] + ROWS[t]]
                        src = quads(bank)[:, :, 0:ROWS[t]]
                    act.activation(dst, src, ACT.Copy).then_inc(turn_evac, 1)
                if place % 2 == 1:
                    tile = place // 2
                    c, t = tile // 3, tile % 3
                    act.wait_ge(qkv_mm, tile + 1)
                    for cols, src in token_parts(PS[4 * (c % 2) + t], t):
                        ins = act.activation(QKV[0:ROWS[t], t, CH * c + cols.start:CH * c + cols.stop], src, ACT.Copy)
                    ins.then_inc(qkv_evac, 1)
                if place == 4:
                    act.wait_ge(dt_arg, 1)
                    act.activation(ECUM, TOEND, ACT.Exp).then_inc(dt_exp, 1)
                    act.wait_ge(dt_w, 1)
                    act.activation(LNW, CUM, ACT.Ln).then_inc(dt_ln, 1)
                if place == 11:
                    act.wait_ge(cum_read, 1)
                    for lo, hi, r in ((0, 2, P), (2, 3, NS)):
                        act.activation(ECUM[0:r, lo:hi, :], CUM[0:r, lo:hi, :], ACT.Exp)
                        act.activation(TOEND[0:r, lo:hi, :], TOEND[0:r, lo:hi, :], ACT.Exp)
                    act.activation(DEC_P, DEC_P, ACT.Exp)
                    act.activation(DEC_S, DEC_S, ACT.Exp).then_inc(cum_exp, 1)

            def decays(u):
                r = ROWS[UNITS[u][0]]
                for half in range(2):
                    act.wait_ge(seg_sub, 2 * u + half + 1)
                    v = SEG[0:r, u % 2, 4 * half:4 * half + 4, 0:r]
                    act.activation(v, v, ACT.Exp).then_inc(seg_exp, 1)

            decays(0)
            for u in range(len(UNITS)):
                if u + 1 < len(UNITS):
                    decays(u + 1)
                t = u % 3
                act.wait_ge(z_mm, u + 1)
                if u >= 2:
                    act.wait_ge(s_z_out[u % 2], 16 * (u // 2))
                for cols, src in token_parts(PS[2 + u % 2], t):
                    ins = act.activation(Z_STAGE[u % 2][0:ROWS[t], cols], src, ACT.Copy)
                ins.then_inc(z_staged, 1)
            for t in range(TILES):
                r = ROWS[t]
                if t == 0:
                    act.wait_ge(sample_y, 1)
                for h in range(RET_HEADS):
                    square_sum(O[0:r, t, RET_DV * h:RET_DV * (h + 1)], r, 4 + 4 * t + h, SQ[0:r, 0:RET_DV])
            act.wait_ge(variance, 2)
            act.activation(RMS[:, 4:16], RMS[:, 4:16], ACT.Sqrt).then_inc(deviation, 1)
            for s in range(2):
                for t in range(TILES):
                    i, r = 3 * s + t, ROWS[t]
                    act.wait_ge(g_mm, i + 1)
                    act.wait_ge(sil_used, i + 1)
                    for cols, src in token_parts(PS[4 * s + t], t):
                        ins = act.activation(SIL[i % 2][0:r, cols], src, ACT.Silu)
                    ins.then_inc(sil_ready, 1)
            for t in range(TILES):
                r = ROWS[t]
                act.wait_ge(s_z_in, 16 * TILES)
                act.activation(Z[0:r, t, :], Z[0:r, t, :], ACT.Silu).then_inc(z_silu, 1)
            for t in range(TILES):
                r = ROWS[t]
                act.wait_ge(z_used, t + 1)
                for g in range(GROUPS):
                    square_sum(XS[0:r, t, GW * g:GW * (g + 1)], r, 16 + 4 * t + g, SQ[0:r, 0:GW])
            act.wait_ge(variance, 3)
            act.activation(RMS[:, 16:28], RMS[:, 16:28], ACT.Sqrt).then_inc(deviation, 1)
            with act.Fori(0, 2) as j:
                for s in range(2):
                    for m in range(4):
                        act.wait_ge(gate_mm, j * 8 + (4 * s + m + 1))
                        act.activation(SG[:, bass.ds(j * 8 + (4 * s + m), 1), :].squeeze(1),
                                       PS[4 * s + m][:, 0:TOKENS], ACT.Sigmoid).then_inc(gate_evac, 1)

        def rms_of(dve, chain, lo, hi, width, nth, n_squares):
            v = RMS[:, lo:hi]
            dve.wait_ge(squares, n_squares)
            dve.tensor_scalar(v, v, 1.0 / width, EPS, ALU.mult, ALU.add).then_inc(variance, 1)
            dve.wait_ge(deviation, nth)
            chain.link(dve.reciprocal(v, v))

        def vector_mixer(dve, chain):
            dve.sem_inc(conv_done, 8)
            dve.sem_inc(upd_evac, 2)
            dve.sem_inc(sil_used, 2)
            dve.sem_inc(ob_evac, 4)
            dve.memset(RMS, 1.0).then_inc(rms_init, 1)
            dve.memset(ZERO, 0.0).then_inc(zero_ready, 1)
            chain.link(dve.memset(DTW, 0.0))
            dve.wait_ge(rms_init, 1)
            rms_of(dve, chain, 0, 3, D_MODEL, 1, 3)
            for t in range(TILES):
                r = ROWS[t]
                dve.tensor_scalar(H[0:r, t, :], X[0:r, t, :], RMS[0:r, t:t + 1], None,
                                  ALU.mult).then_inc(h_ready, 1)
            dve.wait_ge(s_par, 32)
            for n in range(6):
                t, k0 = n // 2, 4 * (n % 2)
                r = ROWS[t]
                dve.wait_ge(h_turned, n + 1)
                dve.tensor_tensor(HT[:, k0:k0 + 4, TOK0[t]:TOK0[t] + r], quads(PS[n])[:, :, 0:r],
                                  heads(norm_mix[:, k0:k0 + 4], 4, r), ALU.mult).then_inc(ht_ready, 1)
            with chain.fori(3, 24) as j:
                for s in range(2):
                    for m in range(4):
                        raw = RAWB[:, s, m, :]
                        raw_s = raw[:, PROMPT_RAW + 1:RAW].rearrange("p (b i) -> p b i", b=DEC_BATCH)
                        mt = bass.ds(j * 8 + (4 * s + m), 1)
                        out = XBC[:, mt, :].squeeze(1)
                        out_s = out[:, SAMPLE].rearrange("p (b i) -> p b i", b=DEC_BATCH)
                        w = conv_w[:, mt, :].squeeze(1)
                        dve.wait_ge(raw_ready, j * 8 + (4 * s + m + 9))
                        dve.wait_ge(pads_ready, j * 8 + (4 * s + m + 1))
                        for i in range(TAPS):
                            for o_, x_ in ((out[:, 0:SEQ], raw[:, i:i + SEQ]), (out_s, raw_s[:, :, i:i + DEC_SEQ])):
                                if i == 0:
                                    ins = dve.tensor_scalar(o_, x_, w[:, 0:1], conv_b[:, mt], ALU.mult, ALU.add)
                                else:
                                    ins = dve.scalar_tensor_tensor(o_, x_, w[:, i:i + 1], o_, ALU.mult, ALU.add)
                            if i < TAPS - 1:
                                chain.link(ins)
                            else:
                                ins.then_inc(conv_done, 1)
            dve.wait_ge(dt_mm, 1)
            for t in range(TILES):
                r = ROWS[t]
                ins = dve.tensor_tensor(DT[0:r, t, :], PS[3][0:r, 32 * t:32 * t + 32], dt_bias[0:r], ALU.add)
            chain.link(ins)
            dve.scalar_tensor_tensor(TOEND, DT, -1.0, DT, ALU.mult, ALU.min).then_inc(dt_arg, 1)
            dve.wait_ge(dt_exp, 1)
            dve.tensor_scalar(CUM, ECUM, 1.0, None, ALU.add).then_inc(dt_w, 1)
            dve.wait_ge(dt_w, 1)
            chain.link(dve.tensor_scalar(TOEND, CUM, -1.0, None, ALU.add))
            chain.link(dve.tensor_tensor(TOEND, ECUM, TOEND, ALU.subtract))
            chain.link(dve.reciprocal(ECUM, CUM))
            chain.link(dve.tensor_tensor(TOEND, TOEND, ECUM, ALU.mult))
            dve.wait_ge(dt_ln, 1)
            chain.link(dve.tensor_tensor(LNW, LNW, TOEND, ALU.add))
            chain.link(dve.scalar_tensor_tensor(DT, DT, 0.0, LNW, ALU.max, ALU.add))
            dve.wait_ge(na_ready, 1)
            dve.scalar_tensor_tensor(DTA, DT, -1.0, NA.unsqueeze(1).to_broadcast([P, TILES, 32]),
                                     ALU.mult, ALU.mult).then_inc(dta_ready, 1)
            def rotate(t):
                r = ROWS[t]
                dve.wait_ge(qkv_evac, 3 + t + 1)
                qk = QKV[0:r, t, 0:1024].rearrange("p (h e n) -> p h e n", h=8, e=2)
                lo, hi = qk[:, :, 0, :], qk[:, :, 1, :]
                cos, sin = (const(n, 64, r, 64 * t).unsqueeze(1).to_broadcast([r, 8, 64]) for n in ("cos", "sin"))
                parts = [ROT[0:r, a, :].rearrange("p (h n) -> p h n", h=8) for a in range(4)]
                for out, a, b in zip(parts, (lo, hi, lo, hi), (cos, sin, sin, cos)):
                    ins = dve.tensor_tensor(out, a, b, ALU.mult)
                chain.link(ins)
                dve.tensor_tensor(lo, parts[0], parts[1], ALU.subtract)
                dve.tensor_tensor(hi, parts[2], parts[3], ALU.add).then_inc(rotated, 1)
                dve.wait_ge(rotated, t + 1)

            rotate(0)
            dve.wait_ge(cum_mm, 1)
            bank = PS[3]
            for lo, hi, r in ((0, 2, P), (2, 3, NS)):
                ins = dve.tensor_copy(CUM[0:r, lo:hi, :],
                                      bank[0:r, 32 * lo:32 * hi].rearrange("p (t h) -> p t h", h=32))
            chain.link(ins)
            for lo, hi, r in ((0, 2, P), (2, 3, NS)):
                dve.tensor_tensor(TOEND[0:r, lo:hi, :],
                                  bank[0:r, 96 + 32 * lo:96 + 32 * hi].rearrange("p (t h) -> p t h", h=32),
                                  CUM[0:r, lo:hi, :], ALU.subtract)
            dve.tensor_copy(DEC_P, bank[:, 128:160])
            dve.tensor_copy(DEC_S, bank[:, 192:448].rearrange("p (b h) -> p b h", h=32)).then_inc(cum_read, 1)
            rotate(1)
            dve.wait_ge(cum_exp, 1)
            for lo, hi, r in ((0, 2, P), (2, 3, NS)):
                ins = dve.tensor_tensor(TOEND[0:r, lo:hi, :], TOEND[0:r, lo:hi, :], DT[0:r, lo:hi, :], ALU.mult)
            ins.then_inc(toend_ready, 1)
            rotate(2)
            dve.wait_ge(turn_evac, 21)
            dve.tensor_tensor(QTD, QKT[:, 0:RET_HEADS, P:TOKENS],
                              const("q_decay", 768).rearrange("p (h n) -> p h n", h=RET_HEADS),
                              ALU.mult).then_inc(qtd_ready, 1)

            def sub(u):
                t, g = UNITS[u]
                r = ROWS[t]
                mask = const("mask_s" if t == 2 else "mask", r, r)
                if u >= 2:
                    dve.wait_ge(back_mm, u - 1)
                for h in range(HPG):
                    if h % 4 == 0:
                        dve.wait_ge(seg_mm, 2 * u + h // 4 + 1)
                    ins = dve.scalar_tensor_tensor(
                        SEG[0:r, u % 2, h, 0:r], quads(PS[h // 4])[0:r, h % 4, 0:r],
                        CUM[0:r, t, HPG * g + h:HPG * g + h + 1], mask, ALU.subtract, ALU.min)
                    if h % 4 == 3:
                        ins.then_inc(seg_sub, 1)

            def weigh(u):
                t, g = UNITS[u]
                r = ROWS[t]
                dve.wait_ge(seg_exp, 2 * u + 2)
                v = SEG[0:r, u % 2, :, 0:r]
                cb = PS[4][0:r, P * (u % 2):P * (u % 2) + r]
                dve.tensor_tensor(v, v, cb.unsqueeze(1).to_broadcast([r, HPG, r]), ALU.mult).then_inc(wts_ready, 1)

            def spread(ap):
                return heads(ap, HPG, HEADDIM)

            def by_head(ap):
                return ap.rearrange("p (h n) -> p h n", h=HPG)

            def take(u):
                t, g = UNITS[u]
                r = ROWS[t]
                cols = slice(GW * g, GW * (g + 1))
                dve.wait_ge(back_mm, u + 1)
                if t == 2:
                    dve.tensor_tensor(XS[0:r, t, cols], XS[0:r, t, cols], PS[5][0:r, :], ALU.add).then_inc(y_evac, 1)
                    return
                chain.link(dve.tensor_tensor(XS[0:r, t, cols], XS[0:r, t, cols], PS[5][0:r, :], ALU.add))
                if t == 1:
                    dve.tensor_tensor(by_head(TMP[0:r, :]), by_head(PS[6][0:r, :]),
                                      spread(ECUM[0:r, t, HPG * g:HPG * (g + 1)]), ALU.mult)
                    chain.link(dve.tensor_tensor(by_head(SSM_PR[:, cols]), by_head(SSM_PR[:, cols]),
                                                 spread(DEC_P[:, HPG * g:HPG * (g + 1)]), ALU.mult))
                    dve.tensor_tensor(XS[0:r, t, cols], XS[0:r, t, cols], TMP[0:r, :], ALU.add)
                    dve.tensor_tensor(SSM_PR[:, cols], SSM_PR[:, cols], PS[7][:, :], ALU.add).then_inc(y_evac, 1)
                else:
                    dve.tensor_copy(SSM_PR[:, cols], PS[7][:, :]).then_inc(y_evac, 1)

            sub(0)
            for u in range(len(UNITS)):
                if u + 1 < len(UNITS):
                    sub(u + 1)
                weigh(u)
                if u >= 1:
                    take(u - 1)
            take(len(UNITS) - 1)

            def decayed(t, bank):
                r = ROWS[t]
                dve.wait_ge(score_mm, t + 1)
                decay = const("decay_s" if t == 2 else "decay", RET_HEADS * r, r)
                dve.tensor_tensor(SM[0:r, :, 0:r], quads(bank)[0:r, :, 0:r],
                                  decay.rearrange("p (h n) -> p h n", h=RET_HEADS), ALU.mult).then_inc(score_ready, 1)

            def o_out(t, banks):
                r = ROWS[t]
                for e in range(2):
                    ins = dve.tensor_copy(O[0:r, t, CH * e:CH * (e + 1)], banks[e][0:r, :])
                return ins

            decayed(0, PS[0])
            dve.wait_ge(ret_mm, 1)
            dve.wait_ge(s_ssm_p, 16)
            o_out(0, (PS[1], PS[2])).then_inc(ret_evac, 1)
            decayed(1, PS[5])
            dve.wait_ge(ret_mm, 2)
            for e in range(2):
                ins = dve.tensor_copy(RET_PR[:, CH * e:CH * (e + 1)], PS[3 + e][:, :])
            ins.then_inc(ret_evac, 1)
            dve.wait_ge(ret_mm, 3)
            o_out(1, (PS[6], PS[7])).then_inc(ret_evac, 1)
            dve.wait_ge(ret_evac, 2)
            dve.wait_ge(ret_mm, 4)
            for h in range(RET_HEADS):
                cols = slice(RET_DV * h, RET_DV * (h + 1))
                ins = dve.scalar_tensor_tensor(RET_PR[:, cols], RET_PR[:, cols], RET_GAMMA[h] ** P,
                                               PS[3 + h // 2][:, RET_DV * (h % 2):RET_DV * (h % 2 + 1)],
                                               ALU.mult, ALU.add)
            ins.then_inc(ret_evac, 1)
            decayed(2, PS[5])

            with chain.fori(DEC_BATCH // 2, 2) as j:
                for p in range(2):
                    dve.wait_ge(cross_mm, j * 2 + (p + 1))
                    for g in range(GROUPS):
                        v = by_head(SSM_IN[p][:, GW * g:GW * (g + 1)])
                        dec = DEC_S[:, bass.ds(j * 2 + p, 1), HPG * g:HPG * (g + 1)].squeeze(1)
                        ins = dve.tensor_tensor(v, v, spread(dec), ALU.mult)
                    chain.link(ins)
                    for u in range(6):
                        bank = PS[6 + u % 2]
                        dve.wait_ge(upd_mm, j * 12 + (6 * p + u + 1))
                        if u < 4:
                            v = SSM_IN[p][:, GW * u:GW * (u + 1)]
                            ins = dve.tensor_tensor(v, v, bank[:, :], ALU.add)
                        else:
                            for e in range(2):
                                h = 2 * (u - 4) + e
                                v = RET_IN[p][:, RET_DV * h:RET_DV * (h + 1)]
                                ins = dve.scalar_tensor_tensor(v, v, RET_GAMMA[h] ** DEC_SEQ,
                                                               bank[:, RET_DV * e:RET_DV * (e + 1)],
                                                               ALU.mult, ALU.add)
                        ins.then_inc(upd_evac, 1)
            dve.wait_ge(closed, 1)
            for g in range(GROUPS):
                cols = slice(GW * g, GW * (g + 1))
                chain.link(dve.tensor_tensor(by_head(TMP[0:NS, :]), by_head(PS[2 + g][0:NS, :]),
                                             spread(ECUM[0:NS, 2, HPG * g:HPG * (g + 1)]), ALU.mult))
                chain.link(dve.tensor_tensor(XS[0:NS, 2, cols], XS[0:NS, 2, cols], TMP[0:NS, :], ALU.add))
            o_out(2, (PS[0], PS[1])).then_inc(sample_y, 1)

            rms_of(dve, chain, 4, 16, RET_DV, 2, 3 + 12)
            for s in range(2):
                for t in range(TILES):
                    i, r = 3 * s + t, ROWS[t]
                    dve.wait_ge(sil_ready, i + 1)
                    for e in range(2):
                        v = O[0:r, t, CH * s + RET_DV * e:CH * s + RET_DV * (e + 1)]
                        col = 4 + 4 * t + 2 * s + e
                        ins = dve.scalar_tensor_tensor(v, v, RMS[0:r, col:col + 1],
                                                       SIL[i % 2][0:r, RET_DV * e:RET_DV * (e + 1)],
                                                       ALU.mult, ALU.mult)
                    ins.then_inc(sil_used, 1)
            for t in range(TILES):
                r = ROWS[t]
                dve.wait_ge(z_silu, t + 1)
                dve.tensor_tensor(XS[0:r, t, :], XS[0:r, t, :], Z[0:r, t, :], ALU.mult).then_inc(z_used, 1)
            rms_of(dve, chain, 16, 28, GW, 3, 15 + 12)
            for t in range(TILES):
                r = ROWS[t]
                for g in range(GROUPS):
                    v = XS[0:r, t, GW * g:GW * (g + 1)]
                    ins = dve.tensor_scalar(v, v, RMS[0:r, 16 + 4 * t + g:17 + 4 * t + g], None, ALU.mult)
                ins.then_inc(y_scaled, 1)
            for n in range(18):
                t, q = (n // 4, n % 4) if n < 12 else ((n - 12) // 2, n % 2)
                r = ROWS[t]
                dve.wait_ge(turn2_mm, n + 1)
                dst, wt = (YT, ssm_norm) if n < 12 else (OT, ret_norm)
                dve.tensor_tensor(dst[:, 4 * q:4 * q + 4, TOK0[t]:TOK0[t] + r], quads(PS[n % 4])[:, :, 0:r],
                                  heads(wt[:, 4 * q:4 * q + 4], 4, r), ALU.mult).then_inc(turn2_evac, 1)
            for n in range(8):
                dve.wait_ge(oa_mm, n + 1)
                dve.tensor_tensor(SG[:, n, :], SG[:, n, :], PS[n][:, 0:TOKENS], ALU.mult).then_inc(oa_evac, 1)
            dve.wait_ge(oa_evac, 8)
            with chain.fori(2, 4) as j:
                for s in range(2):
                    for m in range(2):
                        i = 2 * s + m
                        dve.wait_ge(ob_mm, j * 4 + (i + 1))
                        a = SG[:, bass.ds(j * 4 + i, 1), :].squeeze(1)
                        b = SG[:, bass.ds(j * 4 + (8 + i), 1), :].squeeze(1)
                        chain.link(dve.tensor_tensor(b, b, PS[4 * s + m][:, 0:TOKENS], ALU.mult))
                        dve.tensor_tensor(MERGED[:, bass.ds(j * 4 + i, 1), :].squeeze(1), a, b,
                                          ALU.add).then_inc(ob_evac, 1)
            for s in range(2):
                for t in range(TILES):
                    r = ROWS[t]
                    dve.wait_ge(out_mm, 3 * s + t + 1)
                    for cols, src in token_parts(PS[4 * s + t], t):
                        v = X[0:r, t, CH * s + cols.start:CH * s + cols.stop]
                        ins = dve.tensor_tensor(v, v, src, ALU.add)
                    ins.then_inc(x1_ready, 1)

        def pool_mixer(pool, chain):
            pool.sem_inc(tails_done, 8)
            pool.wait_ge(s_par, 32)
            pool.memset(RAWB[:, :, :, 0:TAPS - 1], 0.0)
            with pool.Fori(0, 3) as j:
                for s in range(2):
                    for m in range(4):
                        raw = RAWB[:, s, m, :]
                        raw_s = raw[:, PROMPT_RAW + 1:RAW].rearrange("p (b i) -> p b i", b=DEC_BATCH)
                        mt = bass.ds(j * 8 + (4 * s + m), 1)
                        pool.wait_ge(conv_done, j * 8 + (4 * s + m + 1))
                        pool.tensor_copy(raw_s[:, :, 0:TAPS - 1],
                                         conv_state[:, mt, :, :].squeeze(1)).then_inc(pads_ready, 1)
                        pool.wait_ge(raw_ready, j * 8 + (4 * s + m + 9))
                        pool.wait_ge(pads_ready, j * 8 + (4 * s + m + 1))
                        pool.tensor_copy(CONV_TAIL[:, mt, :].squeeze(1), raw[:, SEQ:SEQ + TAPS - 1])
                        pool.tensor_copy(CONV_TAIL_S[:, mt, :, :].squeeze(1),
                                         raw_s[:, :, DEC_SEQ:DEC_SEQ + TAPS - 1]).then_inc(tails_done, 1)
            pool.wait_ge(toend_ready, 1)
            for u, (t, g) in enumerate(UNITS):
                r = ROWS[t]
                cols = slice(GW * g, GW * (g + 1))
                hs = slice(HPG * g, HPG * (g + 1))
                if u == 0:
                    pool.wait_ge(turn_evac, turns_to("x", 11))
                if u >= 4:
                    pool.wait_ge(back_mm, u - 3)

                def by_head(ap):
                    return ap.rearrange("p (h n) -> p h n", h=HPG)

                x = by_head(XS[0:r, t, cols])
                pool.tensor_tensor(by_head(XDT[0:r, cols]), x, heads(DT[0:r, t, hs], HPG, HEADDIM), ALU.mult)
                chain.link(pool.tensor_tensor(by_head(XEND[0:r, cols]), x, heads(TOEND[0:r, t, hs], HPG, HEADDIM),
                                              ALU.mult))
                pool.tensor_tensor(x, x, heads(d_skip[0:r, hs], HPG, HEADDIM), ALU.mult).then_inc(xdt_ready, 1)
            for t in range(TILES):
                r = ROWS[t]
                if t == 0:
                    pool.wait_ge(rotated, 3)
                    pool.wait_ge(turn_evac, 21)
                else:
                    pool.wait_ge(ret_mm, 2 * t)
                pool.tensor_tensor(KDEC[0:r, :].rearrange("p (h n) -> p h n", h=RET_HEADS),
                                   QKV[0:r, t, 512:1024].rearrange("p (h n) -> p h n", h=RET_HEADS),
                                   heads(const("k_decay_s" if t == 2 else "k_decay", RET_HEADS, r), RET_HEADS, P),
                                   ALU.mult).then_inc(kdec_ready, 1)
            pool.wait_ge(kdec_ready, 3)
            pool.wait_ge(seg_exp, 24)
            pool.wait_ge(back_mm, 12)
            for p in range(2):
                pool.wait_ge(s_z_out[p], 16 * 6)
            for j in range(DEC_BATCH // 2):
                for p in range(2):
                    b = 2 * j + p
                    if b >= 2:
                        pool.wait_ge(upd_mm, 6 * (b - 1))
                    cols = const("seq_cols", NS, P, NS * b).unsqueeze(1).to_broadcast([P, 4, NS])
                    row = const("seq_rows", 1, NS, b).to_broadcast([NS, 512])
                    pool.tensor_tensor(CTM[p], XBC[:, 20:24, SAMPLE], cols, ALU.mult)
                    pool.tensor_tensor(QTM[p], QTD[:, :, P:], cols, ALU.mult)
                    pool.tensor_tensor(BM[p], BTOK[0:NS, 2, :], row, ALU.mult)
                    pool.tensor_tensor(KM[p], KDEC[0:NS, :], row, ALU.mult).then_inc(masks_ready, 1)

        WG, WL, WD = (region(8192 * n, 8192).rearrange("p (k n) -> p k n", k=KT) for n in range(3))
        BIAS_F32 = region(24576, 3072)
        BIAS = region(37120, 1536).bitcast(BF16)
        NF = region(36096, 1024)
        H2 = region(27648, 3072).rearrange("p (t n) -> p t n", t=TILES)
        H2T = region(30720, 2560).rearrange("p (k n) -> p k n", k=KT)
        CMP = region(33280, BLOCK_COLS * N_EXPERTS).rearrange("p (b e) -> p b e", e=N_EXPERTS)
        XG, ACTB, YB, GLU, LIN, SILU = (region(24576 + 512 * n, 512) for n in range(6))
        XTE, ACTT = (region(27648 + 512 * n, 512).rearrange("p (k h n) -> p k h n", k=4, h=2) for n in range(2))
        SELB = region(35008, LANES // 2).bitcast(BF16)
        YS = region(0, 12288).rearrange("p (t n) -> p t n", t=TILES)
        OUT = region(12288, 3072).rearrange("p (t n) -> p t n", t=TILES)
        SQ_END = region(16384, 1024)

        o = 0

        def temp(n):
            nonlocal o
            o += n
            assert o <= 4608
            return TEMPS[:, o - n:o]

        def tiles(ap, n):
            return ap.rearrange("p (t n) -> p t n", n=n)

        LOG = tiles(temp(96), 32)
        TOP8 = tiles(temp(24), 8)
        IDX8 = tiles(temp(24).bitcast(U32), 8)
        IDX8F = tiles(temp(24), 8)
        CHOSEN = temp(384).rearrange("p (t k e) -> p t k e", t=TILES, k=TOP_K)
        TAKEN = tiles(temp(96), 32)
        RANK = tiles(temp(96), 32)
        RANK_DIV = tiles(temp(96), 32)
        LANE = tiles(temp(96), 32)
        BLOCK = tiles(temp(96), 32)
        COUNT = temp(32)
        BLOCKS_OF = temp(32)
        BLOCKS_TO = temp(32)
        FIRST_BLOCK = temp(32)
        PICKED = temp(384).rearrange("p (t k e) -> p t k e", t=TILES, k=TOP_K)
        LANE_K = tiles(temp(12), 4)
        BLOCK_K = tiles(temp(12), 4)
        GATE = tiles(temp(12), 4)
        GSUM = temp(3)
        IN_LANE = temp(1536).rearrange("p (t k n) -> p t k n", t=TILES, k=TOP_K)
        IN_BLOCK = temp(12 * BLOCK_COLS).rearrange("p (t k n) -> p t k n", t=TILES, k=TOP_K)
        EXPERT_F = temp(BLOCK_COLS)
        EXPERT = temp(BLOCK_COLS).bitcast(I32)
        N_BLOCKS = temp(1).bitcast(I32)
        SELECT = temp(BLOCK_COLS + 1).bitcast(BF16)
        EMPTY = temp(BLOCK_COLS)
        ASSIGN = temp(BLOCK_COLS).bitcast(I32)
        TOKEN = temp(BLOCK_COLS).bitcast(I32)
        GATHER_AT = temp(1).bitcast(I32)
        SCATTER_AT = temp(1).bitcast(I32)

        h2_dram = nc.dram_tensor("normalized_rows", (TOKENS, D_MODEL), F32).ap()
        ys_dram = nc.dram_tensor("assignment_rows", (TOKENS * TOP_K, D_MODEL), F32).ap()

        s_bias, s_nf, s_h2, s_ys = sem("biases_in"), sem("norm_final_in"), sem("h2_out"), sem("rows_in")
        s_wg, s_wl, s_wd = ([sem(f"weights_{w}{n}_in") for n in range(2)] for w in ("gate", "linear", "down"))
        gathered, scattered, s_y = sem("gathered"), sem("scattered"), sem("y_out_done")
        bias_ready, h2_ready, turn3_mm, h2t_ready, logits_mm = (
            sem("bias_ready"), sem("h2_ready"), sem("turn3_mm"), sem("h2t_ready"), sem("logits_mm"))
        taken_ready, rank_mm, places_ready, lists_mm, lists_ready = (
            sem("taken_ready"), sem("rank_mm"), sem("places_ready"), sem("lists_mm"), sem("lists_ready"))
        gate_arg, gate_exp = sem("gate_arg"), sem("gate_exp")
        g_up_mm, lin_mm, y_mm, act_turned, x_turned = (
            sem("g_up_mm"), sem("lin_mm"), sem("y_mm"), sem("act_turned"), sem("x_turned"))
        x_ready, glu_ready, silu_ready, act_ready, actt_ready = (
            sem("x_ready"), sem("glu_ready"), sem("silu_ready"), sem("act_ready"), sem("actt_ready"))
        y_ready, select_ready, end_sum = sem("y_ready"), sem("select_ready"), sem("end_sum")
        out_ready = sem("out_ready")
        index_set, slot_free = sem("index_set"), sem("slot_free")
        G_BANK, L_BANK, TURN_BANK, X_BANK, Y_BANK = PS[1], PS[2], PS[3], PS[4], PS[5]

        def halves(bank):
            return bank[:, :].rearrange("p (k h n) -> p k h n", k=4, h=2)

        def sync_experts(sp):
            sp.wait_ge(turn2_evac, 18)
            for n in range(3):
                rows = slice(32 * n, 32 * n + 32)
                sp.dma_start(BIAS_F32[rows, 0:2 * D_FF], b_gate_up).then_inc(s_bias, 16)
                sp.dma_start(BIAS_F32[rows, 2 * D_FF:3 * D_FF], b_down).then_inc(s_bias, 16)
            sp.dma_start(NF, norm_final.to_broadcast([P, D_MODEL])).then_inc(s_nf, 16)
            sp.wait_ge(ob_evac, 4 + 8)
            for n in range(2):
                sp.dma_start(WL[:, 4 * n:4 * n + 4, :], w_gate_up[0, :, D_FF:2 * D_FF].rearrange(
                    "(k p) n -> p k n", p=P)[:, 4 * n:4 * n + 4, :]).then_inc(s_wl[n], 16)
                sp.dma_start(WD[:, 4 * n:4 * n + 4, :], w_down[0].rearrange(
                    "(k p) n -> p k n", p=P)[:, 4 * n:4 * n + 4, :]).then_inc(s_wd[n], 16)
            sp.wait_ge(out_mm, 6)
            for n in range(2):
                sp.dma_start(WG[:, 4 * n:4 * n + 4, :], w_gate_up[0, :, 0:D_FF].rearrange(
                    "(k p) n -> p k n", p=P)[:, 4 * n:4 * n + 4, :]).then_inc(s_wg[n], 16)
            sp.wait_ge(h2_ready, TILES)
            sp.dma_start(h2_dram[0:SEQ, :].rearrange("(t p) d -> p t d", p=P), H2[:, 0:2, :]).then_inc(s_h2, 16)
            sp.dma_start(h2_dram[SAMPLE, :], H2[0:NS, 2, :]).then_inc(s_h2, 16)

            def load_up(e, w, first, s_in):
                src = w_gate_up[bass.ds(e, 1), :, first:first + D_FF].squeeze(0).rearrange("(k p) n -> p k n", p=P)
                for n in range(2):
                    sp.dma_start(w[:, 4 * n:4 * n + 4, :], src[:, 4 * n:4 * n + 4, :]).then_inc(s_in[n], 16)

            def load_down(e):
                src = w_down[bass.ds(e, 1), :, :].squeeze(0).rearrange("(k p) n -> p k n", p=P)
                for n in range(2):
                    sp.dma_start(WD[:, 4 * n:4 * n + 4, :], src[:, 4 * n:4 * n + 4, :]).then_inc(s_wd[n], 16)

            def next_weights(changed, load, s_in):
                with sp.If(changed):
                    load()
                with sp.Else():
                    for n in range(2):
                        sp.sem_inc(s_in[n], 16)

            sp.wait_ge(lists_ready, 1)
            n_blocks = sp.value_load(N_BLOCKS[0:1, 0:1], min_val=MIN_BLOCKS, max_val=MAX_BLOCKS)
            with sp.Fori(0, n_blocks - 1) as i:
                this = sp.value_load(EXPERT[0:1, bass.ds(i, 1)], min_val=0, max_val=N_EXPERTS - 1)
                e = sp.value_load(EXPERT[0:1, bass.ds(i + 1, 1)], min_val=0, max_val=N_EXPERTS - 1)
                sp.wait_ge(g_up_mm, i + 1)
                sp.sem_inc(slot_free, 1)
                next_weights(e != this, lambda: load_up(e, WG, 0, s_wg), s_wg)
                sp.wait_ge(lin_mm, i + 1)
                sp.sem_inc(slot_free, 1)
                next_weights(e != this, lambda: load_up(e, WL, D_FF, s_wl), s_wl)
                sp.wait_ge(y_mm, i + 1)
                sp.sem_inc(slot_free, 1)
                next_weights(e != this, lambda: load_down(e), s_wd)
            sp.wait_ge(scattered, n_blocks * 16)
            for t in range(TILES):
                r = ROWS[t]
                sp.dma_start(YS[0:r, t, :], ys_dram[TOK0[t] * TOP_K:(TOK0[t] + r) * TOP_K, :].rearrange(
                    "(p k) d -> p (k d)", k=TOP_K)).then_inc(s_ys, 16)
            for t in range(TILES):
                r = ROWS[t]
                sp.wait_ge(out_ready, t + 1)
                sp.dma_start(y_out[TOK0[t]:TOK0[t] + r, :], OUT[0:r, t, :]).then_inc(s_y, 16)
            sp.wait_ge(s_y, 16 * TILES)

        def tensor_experts(pe):
            ident = const("ident", P)
            for n in range(6):
                t, k0 = n // 2, 4 * (n % 2)
                r = ROWS[t]
                pe.wait_ge(h2_ready, t + 1)
                for k in range(4):
                    mm = pe.transpose(quads(PS[n])[:, k, 0:r], H2[0:r, t, P * (k0 + k):P * (k0 + k + 1)],
                                      const("ident", r, r))
                mm.then_inc(turn3_mm, 1)
            for t in range(TILES):
                r = ROWS[t]
                pe.wait_ge(h2t_ready, 6)
                for k in range(KT):
                    mm = pe.matmul(PS[5 + t][0:r, 0:32], H2T[:, k, TOK0[t]:TOK0[t] + r], WR[:, k, :],
                                   start=(k == 0), stop=(k == KT - 1))
                mm.then_inc(logits_mm, 1)
            pe.wait_ge(taken_ready, 1)
            for t in range(TILES):
                r = ROWS[t]
                for s in range(t + 1):
                    lhs = const("before", r, r) if s == t else const("ones", r, P)
                    pe.matmul(PS[7][0:r, 32 * t:32 * t + 32], lhs, TAKEN[0:ROWS[s], s, :],
                              start=(s == 0), stop=(s == t))
            for s in range(TILES):
                mm = pe.matmul(PS[7][:, 96:128], const("ones", P, ROWS[s]), TAKEN[0:ROWS[s], s, :],
                               start=(s == 0), stop=(s == TILES - 1))
            mm.then_inc(rank_mm, 1)
            pe.wait_ge(places_ready, 1)
            for t in range(TILES):
                r = ROWS[t]
                for k in range(TOP_K):
                    mm = pe.matmul(PS[0][:, 0:BLOCK_COLS], IN_LANE[0:r, t, k, :], IN_BLOCK[0:r, t, k, :],
                                   start=(t + k == 0), stop=(t == TILES - 1 and k == TOP_K - 1))
            mm.then_inc(lists_mm, 1)

            def turn(src, bank, done):
                for k in range(4):
                    mm = pe.transpose(quads(bank)[:, k, :], src[:, P * k:P * (k + 1)], ident)
                mm.then_inc(done, 1)

            def by_halves(bank, turned, w, s_in, done, bias_at, i):
                for h in range(2):
                    at = bias_at + CH * h
                    pe.matmul(bank[LANES * h:LANES * (h + 1), :], SELB[0:96, :], BIAS[0:96, at:at + CH],
                              start=True, stop=False, tile_position=(0, LANES * h))
                for k in range(KT):
                    if k % 4 == 0:
                        pe.wait_ge(s_in[k // 4], i * 16 + 16)
                    for h in range(2):
                        mm = pe.matmul(bank[LANES * h:LANES * (h + 1), :], turned[:, k % 4, k // 4, :],
                                       w[:, k, CH * h:CH * (h + 1)], start=False, stop=(k == KT - 1),
                                       tile_position=(0, LANES * h))
                mm.then_inc(done, 1)

            pe.wait_ge(lists_ready, 1)
            n_blocks = pe.value_load(N_BLOCKS[0:1, 0:1], min_val=MIN_BLOCKS, max_val=MAX_BLOCKS)
            pe.wait_ge(bias_ready, 1)
            pe.wait_ge(gathered, 16)
            turn(XG, X_BANK, x_turned)
            with pe.Fori(0, n_blocks) as i:
                pe.wait_ge(select_ready, i + 1)
                pe.wait_ge(x_ready, i + 1)
                by_halves(G_BANK, XTE, WG, s_wg, g_up_mm, 0, i)
                by_halves(L_BANK, XTE, WL, s_wl, lin_mm, D_FF, i)
                pe.wait_ge(gathered, i * 16 + 32)
                turn(XG, X_BANK, x_turned)
                pe.wait_ge(act_ready, i + 1)
                turn(ACTB, TURN_BANK, act_turned)
                pe.wait_ge(y_ready, i + 1)
                pe.wait_ge(actt_ready, i + 1)
                by_halves(Y_BANK, ACTT, WD, s_wd, y_mm, 2 * D_FF, i)

        def scalar_experts(act, chain):
            for t in range(TILES):
                r = ROWS[t]
                act.wait_ge(x1_ready, 3 + t + 1)
                act.wait_ge(squares, 27 + t)
                act.activation(SQ[0:r, :], X[0:r, t, :], ACT.Square,
                               accum_out=RMS[0:r, 28 + t:29 + t]).then_inc(squares, 1)
            act.wait_ge(variance, 4)
            act.activation(RMS[:, 28:31], RMS[:, 28:31], ACT.Sqrt).then_inc(deviation, 1)
            act.wait_ge(gate_arg, 1)
            act.activation(GATE, GATE, ACT.Exp).then_inc(gate_exp, 1)
            act.wait_ge(lists_ready, 1)
            n_blocks = act.value_load(N_BLOCKS[0:1, 0:1], min_val=MIN_BLOCKS, max_val=MAX_BLOCKS)

            def activate(b):
                act.wait_ge(glu_ready, b + 1)
                act.activation(SILU, GLU, ACT.Silu, scale=ALPHA).then_inc(silu_ready, 1)
                act.wait_ge(act_turned, b + 1)
                act.activation(ACTT, halves(TURN_BANK), ACT.Copy, scale=1.0 / ALPHA).then_inc(actt_ready, 1)
                act.wait_ge(y_mm, b + 1)

            activate(0)
            act.activation(YB, Y_BANK[:, :], ACT.Copy).then_inc(y_ready, 1)
            with act.Fori(0, n_blocks - 1) as i:
                activate(i + 1)
                act.wait_ge(scattered, i * 16 + 16)
                act.activation(YB, Y_BANK[:, :], ACT.Copy).then_inc(y_ready, 1)
            for t in range(TILES):
                r = ROWS[t]
                act.wait_ge(end_sum, TOP_K * (t + 1))
                act.wait_ge(squares, 30 + t)
                act.activation(SQ_END[0:r, :], X[0:r, t, :], ACT.Square,
                               accum_out=RMS[0:r, 28 + t:29 + t]).then_inc(squares, 1)
                act.wait_ge(variance, 5 + t)
                act.activation(RMS[:, 28 + t:29 + t], RMS[:, 28 + t:29 + t], ACT.Sqrt).then_inc(deviation, 1)

        def vector_experts(dve, chain):
            dve.sem_inc(y_ready, 1)
            rms_of(dve, chain, 28, 31, D_MODEL, 4, 30)
            for t in range(TILES):
                r = ROWS[t]
                dve.tensor_scalar(H2[0:r, t, :], X[0:r, t, :], RMS[0:r, 28 + t:29 + t], None,
                                  ALU.mult).then_inc(h2_ready, 1)
            for n in range(6):
                t, k0 = n // 2, 4 * (n % 2)
                r = ROWS[t]
                dve.wait_ge(turn3_mm, n + 1)
                dve.tensor_tensor(H2T[:, k0:k0 + 4, TOK0[t]:TOK0[t] + r], quads(PS[n])[:, :, 0:r],
                                  heads(norm_ffn[:, k0:k0 + 4], 4, r), ALU.mult).then_inc(h2t_ready, 1)
            dve.memset(RANK, 0.0)
            chain.link(dve.memset(CHOSEN, 0.0))
            for t in range(TILES):
                r = ROWS[t]
                dve.wait_ge(logits_mm, t + 1)
                chain.link(dve.tensor_tensor(LOG[0:r, t, :], PS[5 + t][0:r, 0:32], b_router[0:r], ALU.add))
                chain.link(dve.max(TOP8[0:r, t, :], LOG[0:r, t, :]))
                chain.link(dve.max_index(IDX8[0:r, t, :], TOP8[0:r, t, :], LOG[0:r, t, :]))
                chain.link(dve.tensor_copy(IDX8F[0:r, t, :], IDX8[0:r, t, :]))
                chain.link(dve.tensor_tensor(
                    CHOSEN[0:r, t, :, :], const("experts", 32, r).unsqueeze(1).to_broadcast([r, TOP_K, N_EXPERTS]),
                    heads(IDX8F[0:r, t, 0:TOP_K], TOP_K, N_EXPERTS), ALU.is_equal))
                ins = dve.tensor_reduce(TAKEN[0:r, t, :], CHOSEN[0:r, t, :, :].rearrange("p k e -> p e k"),
                                        AX.X, ALU.add)
                if t < TILES - 1:
                    chain.link(ins)
                else:
                    ins.then_inc(taken_ready, 1)
            for t in range(TILES):
                r = ROWS[t]
                ins = dve.tensor_scalar(GATE[0:r, t, :], TOP8[0:r, t, 0:TOP_K], TOP8[0:r, t, 0:1], None,
                                        ALU.subtract)
            dve.tensor_scalar(GATE[NS:P, 2, :], RMS[NS:P, 0:TOP_K], 0.0, None, ALU.mult).then_inc(gate_arg, 1)
            dve.wait_ge(rank_mm, 1)
            dve.tensor_copy(RANK[:, 0:2, :], PS[7][:, 0:64].rearrange("p (t e) -> p t e", t=2))
            dve.tensor_copy(RANK[0:NS, 2, :], PS[7][0:NS, 64:96])
            chain.link(dve.tensor_copy(COUNT, PS[7][:, 96:128]))
            dve.tensor_scalar(BLOCKS_OF, COUNT, 0.0, None, ALU.is_gt)
            chain.link(dve.tensor_scalar(RANK_DIV, RANK, float(LANES), None, ALU.is_ge))
            for n in range(1, -(-TOKENS // LANES)):
                if n > 1:
                    dve.scalar_tensor_tensor(RANK_DIV, RANK, float(LANES * n), RANK_DIV, ALU.is_ge, ALU.add)
                chain.link(dve.scalar_tensor_tensor(BLOCKS_OF, COUNT, float(LANES * n), BLOCKS_OF, ALU.is_gt, ALU.add))
            chain.link(dve.tensor_scalar(BLOCKS_OF[:, 0:1], BLOCKS_OF[:, 0:1], 1.0, None, ALU.max))
            chain.link(dve.tensor_tensor_scan(BLOCKS_TO, const("ones", N_EXPERTS), BLOCKS_OF, 0.0,
                                              ALU.mult, ALU.add))
            chain.link(dve.tensor_tensor(FIRST_BLOCK, BLOCKS_TO, BLOCKS_OF, ALU.subtract))
            dve.scalar_tensor_tensor(LANE, RANK_DIV, -float(LANES), RANK, ALU.mult, ALU.add)
            chain.link(dve.tensor_tensor(BLOCK, RANK_DIV, FIRST_BLOCK.unsqueeze(1).to_broadcast([P, TILES, 32]),
                                         ALU.add))
            for src, dst in ((LANE, LANE_K), (BLOCK, BLOCK_K)):
                for t in range(TILES):
                    ins = dve.tensor_tensor(PICKED[:, t, :, :], CHOSEN[:, t, :, :],
                                            src[:, t, :].unsqueeze(1).to_broadcast([P, TOP_K, N_EXPERTS]), ALU.mult)
                chain.link(ins)
                chain.link(dve.tensor_reduce(dst, PICKED, AX.X, ALU.add))
            for t in range(TILES):
                dve.tensor_tensor(IN_LANE[:, t, :, :], const("lanes", P).unsqueeze(1).to_broadcast([P, TOP_K, P]),
                                  heads(LANE_K[:, t, :], TOP_K, P), ALU.is_equal)
                ins = dve.tensor_tensor(IN_BLOCK[:, t, :, :],
                                        const("blocks", BLOCK_COLS).unsqueeze(1).to_broadcast([P, TOP_K, BLOCK_COLS]),
                                        heads(BLOCK_K[:, t, :], TOP_K, BLOCK_COLS), ALU.is_equal)
            chain.link(ins)
            for t in range(TILES):
                ins = dve.tensor_tensor(IN_BLOCK[:, t, :, :], IN_BLOCK[:, t, :, :],
                                        heads(const("assign", TOP_K, P, TOP_K * t), TOP_K, BLOCK_COLS), ALU.mult)
            ins.then_inc(places_ready, 1)
            chain.link(dve.tensor_tensor(CMP, BLOCKS_TO.unsqueeze(1).to_broadcast([P, BLOCK_COLS, N_EXPERTS]),
                                         heads(const("blocks", BLOCK_COLS), BLOCK_COLS, N_EXPERTS), ALU.is_le))
            chain.link(dve.tensor_reduce(EXPERT_F, CMP, AX.X, ALU.add))
            dve.tensor_scalar(SELECT[0:96, 0:BLOCK_COLS], EXPERT_F[0:96, :], const("mod32", 1, 96), None,
                              ALU.is_equal)
            dve.tensor_scalar(EXPERT[0:1, :], EXPERT_F[0:1, :], float(N_EXPERTS - 1), None, ALU.min)
            dve.tensor_copy(N_BLOCKS[0:1, :], BLOCKS_TO[0:1, N_EXPERTS - 1:N_EXPERTS])
            dve.wait_ge(lists_mm, 1)
            chain.link(dve.tensor_scalar(EMPTY, PS[0][:, 0:BLOCK_COLS], 0.0, NOWHERE, ALU.is_equal, ALU.mult))
            chain.link(dve.scalar_tensor_tensor(ASSIGN, PS[0][:, 0:BLOCK_COLS], -1.0, EMPTY, ALU.add, ALU.add))
            chain.link(dve.tensor_scalar(TOKEN, ASSIGN, 2, None, ALU.logical_shift_right))
            for v in (ASSIGN, TOKEN):
                ins = dve.tensor_scalar(v, v, 2.0, const("half", 1), ALU.mult, ALU.add)
            ins.then_inc(lists_ready, 1)
            dve.wait_ge(gate_exp, 1)
            chain.link(dve.tensor_reduce(GSUM, GATE, AX.X, ALU.add))
            chain.link(dve.reciprocal(GSUM, GSUM))
            chain.link(dve.tensor_tensor(GATE, GATE, heads(GSUM, TILES, TOP_K), ALU.mult))

            def x_out(done):
                dve.wait_ge(x_turned, done + 1)
                weight = norm_ffn.rearrange("p (h k) -> p k h", h=2).unsqueeze(3).to_broadcast([P, 4, 2, LANES])
                dve.tensor_tensor(XTE, halves(X_BANK), weight, ALU.mult).then_inc(x_ready, 1)

            dve.wait_ge(lists_ready, 1)
            n_blocks = dve.value_load(N_BLOCKS[0:1, 0:1], min_val=MIN_BLOCKS, max_val=MAX_BLOCKS)
            dve.tensor_copy(SELB[0:96, :], SELECT[0:96, 0:1].to_broadcast([96, LANES])).then_inc(select_ready, 1)
            x_out(0)
            with chain.fori(n_blocks, 1) as i:
                dve.wait_ge(g_up_mm, i + 1)
                dve.tensor_scalar(GLU, G_BANK[:, :], LIMIT, None, ALU.min).then_inc(glu_ready, 1)
                dve.wait_ge(lin_mm, i + 1)
                chain.link(dve.tensor_scalar(LIN, L_BANK[:, :], LIMIT, -LIMIT, ALU.min, ALU.max))
                dve.wait_ge(silu_ready, i + 1)
                dve.scalar_tensor_tensor(ACTB, LIN, 1.0, SILU, ALU.add, ALU.mult).then_inc(act_ready, 1)
                x_out(i + 1)
                dve.wait_ge(y_mm, i + 1)
                dve.tensor_copy(SELB[0:96, :],
                                SELECT[0:96, bass.ds(i + 1, 1)].to_broadcast([96, LANES])).then_inc(select_ready, 1)
            dve.wait_ge(s_nf, 16)
            for t in range(TILES):
                r = ROWS[t]
                dve.wait_ge(s_ys, 16 * TILES)
                for k in range(TOP_K):
                    dve.scalar_tensor_tensor(X[0:r, t, :], YS[0:r, t, D_MODEL * k:D_MODEL * (k + 1)],
                                             GATE[0:r, t, k:k + 1], X[0:r, t, :],
                                             ALU.mult, ALU.add).then_inc(end_sum, 1)
                    dve.wait_ge(end_sum, TOP_K * t + k + 1)
                rms_of(dve, chain, 28 + t, 29 + t, D_MODEL, 5 + t, 31 + t)
                dve.scalar_tensor_tensor(OUT[0:r, t, :], X[0:r, t, :], RMS[0:r, 28 + t:29 + t], NF[0:r, :],
                                         ALU.mult, ALU.mult).then_inc(out_ready, 1)

        def pool_experts(pool, chain):
            pool.wait_ge(s_bias, 96)
            parts = [slice(32 * n, 32 * n + 32) for n in range(3)]
            chain.link(pool.tensor_copy(BIAS[0:96, :], BIAS_F32[0:96, :]))
            for n in range(1, 3):
                for m in range(n, 3):
                    ins = pool.tensor_tensor(BIAS_F32[parts[m], :], BIAS_F32[parts[m], :], BIAS[parts[m], :],
                                             ALU.subtract)
                chain.link(ins)
                for m in range(n, 3):
                    ins = pool.tensor_copy(BIAS[parts[m], :], BIAS_F32[parts[m], :])
                chain.link(ins)
            pool.memset(XG, 0.0).then_inc(bias_ready, 1)
            pool.wait_ge(lists_ready, 1)
            n_blocks = pool.value_load(N_BLOCKS[0:1, 0:1], min_val=MIN_BLOCKS, max_val=MAX_BLOCKS)

            def gather(col):
                chain.link(pool.tensor_copy(GATHER_AT, TOKEN[:, col]))
                pool.sem_inc(index_set, 1)
                pool.indirect_dma_start(out=XG, out_offset=None, in_=h2_dram.rearrange("t (h n) -> (t h) n", h=2),
                                        in_offset=bass.IndirectOffsetOnAxis(ap=GATHER_AT, axis=0),
                                        bounds_check=2 * TOKENS - 1, oob_is_err=False).then_inc(gathered, 16)

            pool.wait_ge(s_h2, 32)
            pool.wait_ge(bias_ready, 1)
            gather(slice(0, 1))
            pool.wait_ge(x_turned, 1)
            gather(slice(1, 2))
            with chain.fori(n_blocks, 2) as i:
                pool.wait_ge(x_turned, i + 2)
                gather(bass.ds(i + 2, 1))
                pool.wait_ge(y_ready, i + 2)
                chain.link(pool.tensor_copy(SCATTER_AT, ASSIGN[:, bass.ds(i, 1)]))
                pool.sem_inc(index_set, 1)
                pool.indirect_dma_start(out=ys_dram.rearrange("t (h n) -> (t h) n", h=2),
                                        out_offset=bass.IndirectOffsetOnAxis(ap=SCATTER_AT, axis=0),
                                        in_=YB, in_offset=None,
                                        bounds_check=2 * TOKENS * TOP_K - 1, oob_is_err=False).then_inc(scattered, 16)

        block = ctx.enter_context(nc.Block())

        @block.sync
        def _(sp):
            sync_mixer(sp)
            sync_experts(sp)

        @block.tensor
        def _(pe):
            tensor_mixer(pe)
            tensor_experts(pe)

        @block.scalar
        def _(act):
            chain = Chain(act, act_order)
            scalar_mixer(act, chain)
            scalar_experts(act, chain)

        @block.vector
        def _(dve):
            chain = Chain(dve, dve_order)
            vector_mixer(dve, chain)
            vector_experts(dve, chain)

        @block.gpsimd
        def _(pool):
            chain = Chain(pool, pool_order)
            pool_mixer(pool, chain)
            pool_experts(pool, chain)


def kernel(**inputs):
    import concourse.bacc as bacc
    from concourse.bass_utils import run_bass_kernel_spmd

    a = {k: np.asarray(v) for k, v in inputs.items()}

    def by_channel(v):
        v = v.reshape(v.shape[:-1] + (v.shape[-1] // P, P))
        return np.moveaxis(np.moveaxis(v, -1, 0), -1, 1)

    arrays = {
        "x_all": np.concatenate([a["x_prompt"][0], a["x_sample"].reshape(NS, D_MODEL)], 0),
        "cst": constants()[0],
        "parc": np.concatenate([by_channel(v).reshape(P, -1) for v in (
            a["conv_w"][0], a["conv_b"][0], a["ssm_norm"][0], a["ret_norm"][0].reshape(-1), a["norm_mix"][0],
            a["norm_ffn"][0], a["state_conv"][0])], 1),
        "rowp": np.concatenate([a["dt_bias"][0], a["a_log"][0], a["d_skip"][0], a["b_router"][0]])[None],
        "norm_final": a["norm_final"][None],
        "w_in": a["w_in"][0],
        "w_out_ret": a["w_out_ret"][0],
        "w_out_ssm": a["w_out_ssm"][0],
        "w_out": a["w_out"][0],
        "w_router": a["w_router"][0],
        "ret_in": a["state_ret"][0],
        "ssm_in": a["state_ssm"][0].reshape(DEC_BATCH, INNER, DSTATE).transpose(0, 2, 1),
        "w_gate_up": a["w_gate_up"][0],
        "b_gate_up": a["b_gate_up"][0],
        "w_down": a["w_down"][0],
        "b_down": a["b_down"][0],
    }
    outs = {
        "y_out": (TOKENS, D_MODEL),
        "ret_p": (RET_HEADS, RET_DK, RET_DV),
        "ret_s": (DEC_BATCH, RET_HEADS, RET_DK, RET_DV),
        "ssm_p": (DSTATE, INNER),
        "ssm_s": (DEC_BATCH, DSTATE, INNER),
        "conv_p": (P, 24, TAPS - 1),
        "conv_s": (P, 24, DEC_BATCH, TAPS - 1),
    }
    nc = bacc.Bacc("TRN2", target_bir_lowering=False, num_devices=1)
    args, sent = [], {}
    for name, v in arrays.items():
        v = np.ascontiguousarray(v)
        sent["in_" + name] = v
        args.append(nc.dram_tensor("in_" + name, v.shape, mybir.dt.from_np(v.dtype), kind="ExternalInput").ap())
    for name, shape in outs.items():
        args.append(nc.dram_tensor("out_" + name, shape, F32, kind="ExternalOutput").ap())
    program(nc, *args)
    got = run_bass_kernel_spmd(nc, [sent], core_ids=[0]).results[0]
    g = {name: np.asarray(got["out_" + name]) for name in outs}

    def ssm_back(v):
        return np.ascontiguousarray(np.swapaxes(v, -1, -2)).reshape(v.shape[:-2] + (SSM_HEADS, HEADDIM, DSTATE))

    return (
        np.ascontiguousarray(g["y_out"][0:SEQ])[None],
        np.ascontiguousarray(g["y_out"][SEQ:]).reshape(DEC_BATCH, DEC_SEQ, D_MODEL),
        g["ret_p"][None, None],
        g["ret_s"][None],
        ssm_back(g["ssm_p"])[None, None],
        ssm_back(g["ssm_s"])[None],
        np.ascontiguousarray(g["conv_p"].transpose(2, 1, 0)).reshape(1, 1, TAPS - 1, CONV_DIM),
        np.ascontiguousarray(g["conv_s"].transpose(2, 3, 1, 0)).reshape(1, DEC_BATCH, TAPS - 1, CONV_DIM),
    )
```
